# Optimizing a Trainium2 kernel written in Bass

```python
import math
import jax, jax.numpy as jnp
from jax import lax
import numpy as np
import jax
import jax.numpy as jnp

D_MODEL = 1024
BATCH = 1
SEQ = 256
DEPTH = 2

CTX_LEN = 256
GRID_W = 64
N_BRANCH = 3
BRANCH_W = D_MODEL // 2
RET_HEADS = 4
RET_DK = BRANCH_W // RET_HEADS
DIFF_HEADS = 4
DIFF_DV = BRANCH_W // DIFF_HEADS
DIFF_DQK = DIFF_DV // 2
MLP_GROUPS = 4
MLP_GW = BRANCH_W // MLP_GROUPS
CHUNK = 128
RET_CHUNK = 128
Q_BLOCK = 128
ROPE_BASE = 10000.0
EPS = 1e-6
KV_SIZES = (BRANCH_W, BRANCH_W, BRANCH_W, BRANCH_W)
REST_SIZES = (BRANCH_W,) * 7 + (N_BRANCH * D_MODEL,)
IN_SIZES = KV_SIZES + REST_SIZES
KV_COLS = 4 * BRANCH_W
IN_COLS = KV_COLS + 7 * BRANCH_W + N_BRANCH * D_MODEL


def rms_norm(x, g=None):
    xf = x.astype(jnp.float32)
    y = xf * lax.rsqrt(jnp.mean(xf * xf, axis=-1, keepdims=True) + EPS)
    if g is not None:
        y = y * g.astype(jnp.float32)
    return y.astype(x.dtype)

def layer_norm(x):
    xf = x.astype(jnp.float32)
    mu = jnp.mean(xf, axis=-1, keepdims=True)
    var = jnp.mean(jnp.square(xf - mu), axis=-1, keepdims=True)
    return ((xf - mu) * lax.rsqrt(var + EPS)).astype(x.dtype)

def modulate(x, g, shift, scale):
    return rms_norm(x, g) * (1.0 + scale) + shift

def split_cols(z, sizes):
    idx = np.cumsum(sizes)[:-1].tolist()
    return jnp.split(z, idx, axis=-1)

def to_heads(t, n_heads):
    b, n, w = t.shape
    return t.reshape(b, n, n_heads, w // n_heads).transpose(0, 2, 1, 3)

def to_diff_heads(t):
    b, n, _ = t.shape
    return t.reshape(b, n, DIFF_HEADS, 2, DIFF_DQK).transpose(0, 2, 3, 1, 4)

def from_heads(t):
    b, h, n, d = t.shape
    return t.transpose(0, 2, 1, 3).reshape(b, n, h * d)

def rope_angles(row_pos, col_pos, head_dim):
    n_freq = head_dim // 4
    inv = ROPE_BASE ** (-jnp.arange(n_freq, dtype=jnp.float32) / n_freq)
    ang = jnp.concatenate([row_pos[:, None] * inv, col_pos[:, None] * inv], axis=-1)
    return jnp.cos(ang), jnp.sin(ang)

def apply_rope(x, cos, sin):
    x1, x2 = jnp.split(x, 2, axis=-1)
    cos = cos.astype(x.dtype)
    sin = sin.astype(x.dtype)
    return jnp.concatenate([x1 * cos - x2 * sin, x1 * sin + x2 * cos], axis=-1)

def retention_chunkwise(q, k, v, log_gamma, state0):
    in_dtype = q.dtype
    q, k, v = q.astype(jnp.float32), k.astype(jnp.float32), v.astype(jnp.float32)
    b, h, n, dk = q.shape
    dv = v.shape[-1]
    nc = n // RET_CHUNK
    qc = q.reshape(b, h, nc, RET_CHUNK, dk)
    kc = k.reshape(b, h, nc, RET_CHUNK, dk)
    vc = v.reshape(b, h, nc, RET_CHUNK, dv)
    pos = jnp.arange(RET_CHUNK, dtype=jnp.float32)
    lg = log_gamma.astype(jnp.float32)[:, None]
    dist = pos[:, None] - pos[None, :]
    d_in = jnp.where(dist >= 0, jnp.exp(lg[:, :, None] * jnp.maximum(dist, 0.0)), 0.0)
    q_dec = jnp.exp(lg * (pos + 1.0))
    k_dec = jnp.exp(lg * (RET_CHUNK - 1.0 - pos))
    chunk_dec = jnp.exp(lg[:, 0] * RET_CHUNK)
    s = jnp.einsum('bhnid,bhnjd->bhnij', qc, kc) * d_in[None, :, None]
    inner = jnp.einsum('bhnij,bhnje->bhnie', s, vc)
    kv = jnp.einsum('bhnjd,hj,bhnje->bhnde', kc, k_dec, vc)

    def step(state, kv_n):
        return chunk_dec[None, :, None, None] * state + kv_n, state

    final, prev = lax.scan(step, state0.astype(jnp.float32), jnp.moveaxis(kv, 2, 0))
    prev = jnp.moveaxis(prev, 0, 2)
    cross = jnp.einsum('bhnid,hi,bhnde->bhnie', qc, q_dec, prev)
    out = (inner + cross).reshape(b, h, n, dv)
    return out.astype(in_dtype), final

def retention_final_state(k, v, log_gamma):
    n = k.shape[2]
    w = jnp.exp(log_gamma[:, None] * (n - 1.0 - jnp.arange(n, dtype=jnp.float32)))
    return jnp.einsum('bhjd,hj,bhje->bhde', k.astype(jnp.float32), w, v.astype(jnp.float32))

def bidir_retention(q, k, v, log_gamma, state_f, state_b):
    out_f, fin_f = retention_chunkwise(q, k, v, log_gamma[0], state_f)
    out_b, fin_b = retention_chunkwise(jnp.flip(q, 2), jnp.flip(k, 2), jnp.flip(v, 2), log_gamma[1], state_b)
    return out_f + jnp.flip(out_b, 2), fin_f, fin_b

def diff_attend(q, k, v, lam):
    s = jnp.einsum('bhmqd,bhmkd->bhmqk', q.astype(jnp.float32), k.astype(jnp.float32)) * (DIFF_DQK ** -0.5)
    p = jax.nn.softmax(s, axis=-1)
    a = p[:, :, 0] - lam * p[:, :, 1]
    return jnp.einsum('bhqk,bhkv->bhqv', a, v.astype(jnp.float32)).astype(v.dtype)

def diff_attend_blocked(q, k, v, lam):
    b, h, _, n, d = q.shape
    nb = n // Q_BLOCK
    qb = jnp.moveaxis(q.reshape(b, h, 2, nb, Q_BLOCK, d), 3, 0)
    o = lax.map(lambda blk: diff_attend(blk, k, v, lam), qb)
    return jnp.moveaxis(o, 0, 2).reshape(b, h, n, -1)

def chunk_mlp(u, v, gate, w_s, b_s):
    b, n, _ = u.shape
    nch = n // CHUNK
    vn = layer_norm(v).reshape(b, nch, CHUNK, MLP_GROUPS, MLP_GW)
    sp = jnp.einsum('gij,bnjgc->bnigc', w_s, vn) + b_s.T[:, :, None]
    return u * sp.reshape(b, n, BRANCH_W) * jax.nn.silu(gate)

def merge_branches(o_ret, o_mlp, o_diff, merge_logits, w_bo, w_o):
    g_ret, g_mlp, g_diff = jnp.split(jax.nn.sigmoid(merge_logits), N_BRANCH, axis=-1)
    y = g_ret * (o_ret @ w_bo[0]) + g_mlp * (o_mlp @ w_bo[1]) + g_diff * (o_diff @ w_bo[2])
    return y @ w_o

def first_inputs(seed: int = 0) -> dict:
    key = jax.random.key(seed)
    ks = jax.random.split(key, 16)
    f32 = jnp.float32
    nrm = jax.random.normal
    x = nrm(ks[0], (BATCH, SEQ, D_MODEL), f32)
    c = nrm(ks[1], (BATCH, D_MODEL), f32)
    ctx = nrm(ks[2], (BATCH, CTX_LEN, D_MODEL), f32)
    c_ctx = nrm(ks[3], (D_MODEL,), f32)
    w_mod = nrm(ks[4], (DEPTH, D_MODEL, 3 * D_MODEL), f32) * (0.5 * D_MODEL ** -0.5)
    b_mod = 0.02 * nrm(ks[5], (DEPTH, 3 * D_MODEL), f32)
    g_pre = 1.0 + 0.05 * nrm(ks[6], (DEPTH, D_MODEL), f32)
    g_post = 1.0 + 0.05 * nrm(ks[7], (DEPTH, D_MODEL), f32)
    w_in = nrm(ks[8], (DEPTH, D_MODEL, IN_COLS), f32) * (D_MODEL ** -0.5)
    base = jnp.log(2.0 ** (5.0 + jnp.arange(RET_HEADS, dtype=f32)) - 1.0)
    ret_decay_logit = base[None, None, :] + 0.1 * nrm(ks[9], (DEPTH, 2, RET_HEADS), f32)
    mlp_w_s = nrm(ks[10], (DEPTH, MLP_GROUPS, CHUNK, CHUNK), f32) * (CHUNK ** -0.5)
    mlp_b_s = 1.0 + 0.1 * nrm(ks[11], (DEPTH, MLP_GROUPS, CHUNK), f32)
    diff_lambda_q = 0.1 * nrm(ks[12], (DEPTH, 2, DIFF_DQK), f32)
    diff_lambda_k = 0.1 * nrm(ks[13], (DEPTH, 2, DIFF_DQK), f32)
    w_branch_out = nrm(ks[14], (DEPTH, N_BRANCH, BRANCH_W, D_MODEL), f32) * (BRANCH_W ** -0.5)
    w_out = nrm(ks[15], (DEPTH, D_MODEL, D_MODEL), f32) * (D_MODEL ** -0.5)
    return {"x": x, "c": c, "ctx": ctx, "c_ctx": c_ctx, "w_mod": w_mod, "b_mod": b_mod,
            "g_pre": g_pre, "g_post": g_post, "w_in": w_in, "ret_decay_logit": ret_decay_logit,
            "mlp_w_s": mlp_w_s, "mlp_b_s": mlp_b_s, "diff_lambda_q": diff_lambda_q,
            "diff_lambda_k": diff_lambda_k, "w_branch_out": w_branch_out, "w_out": w_out}

def first_block(x, c, ctx, c_ctx, w_mod, b_mod, g_pre, g_post, w_in, ret_decay_logit,
              mlp_w_s, mlp_b_s, diff_lambda_q, diff_lambda_k, w_branch_out, w_out):
    b = x.shape[0]
    n_lat = x.shape[1]
    rows = n_lat // GRID_W
    row_pos = jnp.repeat(jnp.arange(rows, dtype=jnp.float32), GRID_W)
    col_pos = jnp.tile(jnp.arange(GRID_W, dtype=jnp.float32), rows)
    cos_r, sin_r = rope_angles(row_pos, col_pos, RET_DK)
    cos_d, sin_d = rope_angles(row_pos, col_pos, DIFF_DQK)
    silu_c = jax.nn.silu(c)
    silu_cc = jax.nn.silu(c_ctx)
    ret_scale = RET_DK ** -0.5

    for l in range(DEPTH):
        last = l == DEPTH - 1
        shift, scale, gate = jnp.split((silu_c @ w_mod[l] + b_mod[l])[:, None, :], 3, axis=-1)
        shift_c, scale_c, gate_c = jnp.split(silu_cc @ w_mod[l] + b_mod[l], 3, axis=-1)
        h = modulate(x, g_pre[l], shift, scale)
        hc = modulate(ctx, g_pre[l], shift_c, scale_c)
        log_gamma = -jax.nn.softplus(-ret_decay_logit[l].astype(jnp.float32))
        lam_init = 0.8 - 0.6 * math.exp(-0.3 * l)
        lam = (jnp.exp(jnp.sum(diff_lambda_q[l, 0] * diff_lambda_k[l, 0]))
               - jnp.exp(jnp.sum(diff_lambda_q[l, 1] * diff_lambda_k[l, 1])) + lam_init).astype(jnp.float32)

        if last:
            c_rk, c_rv, c_dk, c_dv = split_cols(hc @ w_in[l][:, :KV_COLS], KV_SIZES)
        else:
            zc = split_cols(hc @ w_in[l], IN_SIZES)
            c_rk, c_rv, c_dk, c_dv = zc[:4]
        crk = to_heads(c_rk, RET_HEADS) * ret_scale
        crv = to_heads(c_rv, RET_HEADS)
        cdk = to_diff_heads(c_dk)
        cdv = to_heads(c_dv, DIFF_HEADS)
        if last:
            s_f = retention_final_state(crk, crv, log_gamma[0])
            s_b = retention_final_state(jnp.flip(crk, 2), jnp.flip(crv, 2), log_gamma[1])
        else:
            c_rq, c_rg, c_dq, c_dg, c_mu, c_mv, c_mg, c_mlog = zc[4:]
            zero = jnp.zeros((b, RET_HEADS, RET_DK, RET_DK), jnp.float32)
            c_ret, s_f, s_b = bidir_retention(to_heads(c_rq, RET_HEADS), crk, crv, log_gamma, zero, zero)
            co_ret = from_heads(rms_norm(c_ret)) * jax.nn.silu(c_rg)
            c_diff = diff_attend(to_diff_heads(c_dq), cdk, cdv, lam)
            co_diff = from_heads(rms_norm(c_diff) * (1.0 - lam_init)) * jax.nn.silu(c_dg)
            co_mlp = chunk_mlp(c_mu, c_mv, c_mg, mlp_w_s[l], mlp_b_s[l])
            c_out = merge_branches(co_ret, co_mlp, co_diff, c_mlog, w_branch_out[l], w_out[l])
            ctx_next = ctx + gate_c * rms_norm(c_out, g_post[l])

        rk_, rv_, dk_, dv_, rq_, rg_, dq_, dg_, mu_, mv_, mg_, mlog_ = split_cols(h @ w_in[l], IN_SIZES)
        rq = apply_rope(to_heads(rq_, RET_HEADS), cos_r, sin_r)
        rk = apply_rope(to_heads(rk_, RET_HEADS), cos_r, sin_r) * ret_scale
        rv = to_heads(rv_, RET_HEADS)
        ret_o, _, _ = bidir_retention(rq, rk, rv, log_gamma, s_f, s_b)
        o_ret = from_heads(rms_norm(ret_o)) * jax.nn.silu(rg_)

        dq = apply_rope(to_diff_heads(dq_), cos_d, sin_d)
        dk = apply_rope(to_diff_heads(dk_), cos_d, sin_d)
        dv = to_heads(dv_, DIFF_HEADS)
        k_all = jnp.concatenate([cdk, dk], axis=3)
        v_all = jnp.concatenate([cdv, dv], axis=2)
        diff_o = diff_attend_blocked(dq, k_all, v_all, lam)
        o_diff = from_heads(rms_norm(diff_o) * (1.0 - lam_init)) * jax.nn.silu(dg_)

        o_mlp = chunk_mlp(mu_, mv_, mg_, mlp_w_s[l], mlp_b_s[l])
        out = merge_branches(o_ret, o_mlp, o_diff, mlog_, w_branch_out[l], w_out[l])
        x = x + gate * rms_norm(out, g_post[l])
        if not last:
            ctx = ctx_next
    return x


HEAD_DIM = 64
SB_HEADS = 8
FOX_HEADS = 8
DSA_HEADS = 8
DSA_KV_HEADS = 2
DSA_GROUP = DSA_HEADS // DSA_KV_HEADS
IDX_HEADS = 4
IDX_DIM = 64
BRANCH_WIDTH = SB_HEADS * HEAD_DIM
D_FF = 4 * D_MODEL
ROPE_THETA = 500000.0
ROT_DIM = HEAD_DIM // 4
TOPK_MAX = 256
NORM_EPS = 1e-6

COL_SIZES = (
    SB_HEADS * HEAD_DIM, SB_HEADS * HEAD_DIM, SB_HEADS * HEAD_DIM,
    FOX_HEADS * HEAD_DIM, FOX_HEADS * HEAD_DIM, FOX_HEADS * HEAD_DIM,
    FOX_HEADS,
    DSA_HEADS * HEAD_DIM, DSA_KV_HEADS * HEAD_DIM, DSA_KV_HEADS * HEAD_DIM,
    IDX_HEADS * IDX_DIM, IDX_DIM, IDX_HEADS,
    N_BRANCH * D_MODEL,
)
COL_TOTAL = sum(COL_SIZES)
COL_SPLITS = tuple(sum(COL_SIZES[:i + 1]) for i in range(len(COL_SIZES) - 1))


def _rmsnorm(x, g):
    xf = x.astype(jnp.float32)
    y = xf * lax.rsqrt(jnp.mean(xf * xf, axis=-1, keepdims=True) + NORM_EPS)
    return (y * g.astype(jnp.float32)).astype(x.dtype)

def _partial_rope(x, positions):
    half = ROT_DIM // 2
    inv_freq = ROPE_THETA ** (-jnp.arange(0, ROT_DIM, 2, dtype=jnp.float32) / ROT_DIM)
    ang = positions.astype(jnp.float32)[:, :, None] * inv_freq
    cos = jnp.cos(ang)[:, :, None, :]
    sin = jnp.sin(ang)[:, :, None, :]
    xf = x.astype(jnp.float32)
    x1, x2, rest = xf[..., :half], xf[..., half:ROT_DIM], xf[..., ROT_DIM:]
    out = jnp.concatenate([x1 * cos - x2 * sin, x2 * cos + x1 * sin, rest], axis=-1)
    return out.astype(x.dtype)

def _to_blocks(a):
    b, s = a.shape[0], a.shape[1]
    return jnp.moveaxis(a.reshape(b, s // Q_BLOCK, Q_BLOCK, *a.shape[2:]), 1, 0)

def _from_blocks(a):
    a = jnp.moveaxis(a, 0, 1)
    return a.reshape(a.shape[0], a.shape[1] * a.shape[2], *a.shape[3:])

def _stick_breaking_attention(q, k, v):
    b, s, h, dh = q.shape
    scale = dh ** -0.5
    kf = k.astype(jnp.float32)
    vf = v.astype(jnp.float32)
    s_idx = jnp.arange(s)
    t_blk = jnp.arange(s).reshape(s // Q_BLOCK, Q_BLOCK)

    def block(args):
        qb, tb = args
        z = jnp.einsum('bthd,bshd->bhts', qb.astype(jnp.float32), kf) * scale
        strict = s_idx[None, :] < tb[:, None]
        log_beta = jax.nn.log_sigmoid(z)
        log_1m = jnp.where(strict, jax.nn.log_sigmoid(-z), 0.0)
        later = lax.cumsum(log_1m, axis=3, reverse=True) - log_1m
        w = jnp.where(strict, jnp.exp(log_beta + later), 0.0)
        return jnp.einsum('bhts,bshd->bthd', w, vf)

    out = lax.map(block, (_to_blocks(q), t_blk))
    return _from_blocks(out).reshape(b, s, h * dh).astype(q.dtype)

def _forgetting_attention(q, k, v, log_f):
    b, s, h, dh = q.shape
    scale = dh ** -0.5
    kf = k.astype(jnp.float32)
    vf = v.astype(jnp.float32)
    c = jnp.cumsum(log_f, axis=1).transpose(0, 2, 1)
    c_blk = jnp.moveaxis(c.reshape(b, h, s // Q_BLOCK, Q_BLOCK), 2, 0)
    s_idx = jnp.arange(s)
    t_blk = jnp.arange(s).reshape(s // Q_BLOCK, Q_BLOCK)

    def block(args):
        qb, cb, tb = args
        z = jnp.einsum('bthd,bshd->bhts', qb.astype(jnp.float32), kf) * scale
        z = z + cb[..., None] - c[:, :, None, :]
        causal = s_idx[None, :] <= tb[:, None]
        p = jax.nn.softmax(jnp.where(causal, z, -jnp.inf), axis=-1)
        return jnp.einsum('bhts,bshd->bthd', p, vf)

    out = lax.map(block, (_to_blocks(q), c_blk, t_blk))
    return _from_blocks(out).reshape(b, s, h * dh).astype(q.dtype)

def _indexed_sparse_attention(q, k, v, q_idx, k_idx, w_idx, top_k):
    b, s, g, r, dh = q.shape
    scale = dh ** -0.5
    kif = k_idx.astype(jnp.float32)
    s_idx = jnp.arange(s)
    t_blk = jnp.arange(s).reshape(s // Q_BLOCK, Q_BLOCK)
    gather = jax.vmap(lambda a, i: a[i])

    def block(args):
        qb, qib, wb, tb = args
        dots = jnp.einsum('bthi,bsi->bths', qib.astype(jnp.float32), kif) * (IDX_DIM ** -0.5)
        score = jnp.einsum('bth,bths->bts', wb.astype(jnp.float32) * (IDX_HEADS ** -0.5),
                           jax.nn.relu(dots))
        causal = s_idx[None, :] <= tb[:, None]
        score = jnp.where(causal[None], score, -jnp.inf)
        _, sel = lax.top_k(score, top_k)
        valid = sel <= tb[None, :, None]
        k_sel = gather(k, sel).astype(jnp.float32)
        v_sel = gather(v, sel).astype(jnp.float32)
        z = jnp.einsum('btgrd,btkgd->btgrk', qb.astype(jnp.float32), k_sel) * scale
        z = jnp.where(valid[:, :, None, None, :], z, -jnp.inf)
        p = jax.nn.softmax(z, axis=-1)
        return jnp.einsum('btgrk,btkgd->btgrd', p, v_sel)

    out = lax.map(block, (_to_blocks(q), _to_blocks(q_idx), _to_blocks(w_idx), t_blk))
    return _from_blocks(out).reshape(b, s, g * r * dh).astype(q.dtype)

def _layer(x, positions, g_mix, w_in, b_forget, w_branch, w_out, g_mlp, w_up, w_down):
    b, s, _ = x.shape
    h = _rmsnorm(x, g_mix)
    proj = h @ w_in
    (qa, ka, va, qb, kb, vb, fl, qc, kc, vc, qi, ki, wi, gl) = jnp.split(proj, COL_SPLITS, axis=-1)

    def heads(a, n):
        return a.reshape(b, s, n, -1)

    br_a = _stick_breaking_attention(heads(qa, SB_HEADS), heads(ka, SB_HEADS), heads(va, SB_HEADS))
    log_f = jax.nn.log_sigmoid((fl + b_forget).astype(jnp.float32))
    br_b = _forgetting_attention(heads(qb, FOX_HEADS), heads(kb, FOX_HEADS),
                                 heads(vb, FOX_HEADS), log_f)
    qc = _partial_rope(heads(qc, DSA_HEADS), positions).reshape(b, s, DSA_KV_HEADS, DSA_GROUP, HEAD_DIM)
    kc = _partial_rope(heads(kc, DSA_KV_HEADS), positions)
    vc = heads(vc, DSA_KV_HEADS)
    qi = _partial_rope(heads(qi, IDX_HEADS), positions)
    ki = _partial_rope(ki[:, :, None, :], positions)[:, :, 0, :]
    top_k = min(TOPK_MAX, s // 4)
    br_c = _indexed_sparse_attention(qc, kc, vc, qi, ki, wi, top_k)

    gates = jax.nn.sigmoid(gl.reshape(b, s, N_BRANCH, D_MODEL))
    y = (gates[:, :, 0, :] * (br_a @ w_branch[0])
         + gates[:, :, 1, :] * (br_b @ w_branch[1])
         + gates[:, :, 2, :] * (br_c @ w_branch[2]))
    x = x + y @ w_out

    h2 = _rmsnorm(x, g_mlp)
    x = x + jnp.square(jax.nn.relu(h2 @ w_up)) @ w_down
    return x

def second_inputs(seed: int = 0) -> dict:
    key = jax.random.key(seed)
    ks = jax.random.split(key, 12)
    f32 = jnp.float32
    x = jax.random.normal(ks[0], (BATCH, SEQ, D_MODEL), f32)
    positions = jnp.broadcast_to(jnp.arange(SEQ, dtype=jnp.int32), (BATCH, SEQ))
    g_mix = 1.0 + 0.02 * jax.random.normal(ks[1], (DEPTH, D_MODEL), f32)
    w_in = jax.random.normal(ks[2], (DEPTH, D_MODEL, COL_TOTAL), f32) * D_MODEL ** -0.5
    b_forget = jax.random.uniform(ks[3], (DEPTH, FOX_HEADS), f32, minval=1.0, maxval=4.0)
    w_branch = jax.random.normal(ks[4], (DEPTH, N_BRANCH, BRANCH_WIDTH, D_MODEL), f32) * BRANCH_WIDTH ** -0.5
    w_out = jax.random.normal(ks[5], (DEPTH, D_MODEL, D_MODEL), f32) * D_MODEL ** -0.5
    g_mlp = 1.0 + 0.02 * jax.random.normal(ks[6], (DEPTH, D_MODEL), f32)
    w_up = jax.random.normal(ks[7], (DEPTH, D_MODEL, D_FF), f32) * D_MODEL ** -0.5
    w_down = jax.random.normal(ks[8], (DEPTH, D_FF, D_MODEL), f32) * D_FF ** -0.5
    g_final = 1.0 + 0.02 * jax.random.normal(ks[9], (D_MODEL,), f32)
    return {'x': x, 'positions': positions, 'g_mix': g_mix, 'w_in': w_in,
            'b_forget': b_forget, 'w_branch': w_branch, 'w_out': w_out,
            'g_mlp': g_mlp, 'w_up': w_up, 'w_down': w_down, 'g_final': g_final}

def second_block(x, positions, g_mix, w_in, b_forget, w_branch, w_out, g_mlp, w_up, w_down, g_final):
    for layer in range(DEPTH):
        x = _layer(x, positions, g_mix[layer], w_in[layer], b_forget[layer], w_branch[layer],
                   w_out[layer], g_mlp[layer], w_up[layer], w_down[layer])
    return _rmsnorm(x, g_final)


def setup_inputs(seed=0):
    out = dict(first_inputs(seed))
    for name, value in second_inputs(seed + 1).items():
        if name != "x":
            out[name + "_2"] = value
    return out


def reference(
    x, c, ctx, c_ctx, w_mod, b_mod, g_pre, g_post, w_in, ret_decay_logit, mlp_w_s, mlp_b_s,
    diff_lambda_q, diff_lambda_k, w_branch_out, w_out, positions_2, g_mix_2, w_in_2, b_forget_2,
    w_branch_2, w_out_2, g_mlp_2, w_up_2, w_down_2, g_final_2,
):
    x = first_block(
        x, c, ctx, c_ctx, w_mod, b_mod, g_pre, g_post, w_in, ret_decay_logit, mlp_w_s, mlp_b_s,
        diff_lambda_q, diff_lambda_k, w_branch_out, w_out,
    )
    return second_block(
        x, positions_2, g_mix_2, w_in_2, b_forget_2, w_branch_2, w_out_2, g_mlp_2, w_up_2,
        w_down_2, g_final_2,
    )


_drawn_inputs = setup_inputs


def setup_inputs(seed=0):
    import zlib

    import numpy as np

    out = dict(_drawn_inputs(seed))
    spreads = {}
    factors = {'diff_lambda_k': 4.013, 'g_mix_2': 2.68, 'g_final_2': 2.712}
    for name, (base, spread) in spreads.items():
        noise = np.random.default_rng([zlib.crc32(name.encode()), seed]).standard_normal(out[name].shape)
        drawn = base * np.exp(spread * noise) if base else spread * noise
        out[name] = jnp.asarray(drawn.astype(out[name].dtype))
    for name, factor in factors.items():
        out[name] = (out[name] * factor).astype(out[name].dtype)
    return out
```

```python
import math
from contextlib import ExitStack, contextmanager

import numpy as np

import concourse.bass as bass
from concourse import mybir

F32, F32R, BF16, I32 = mybir.dt.float32, mybir.dt.float32r, mybir.dt.bfloat16, mybir.dt.int32
ACT, ALU, AX = mybir.ActivationFunctionType, mybir.AluOpType, mybir.AxisListType

P = 128
D = 1024
S = 256
TT = S // P
KT = D // P
CH = 512
SLAB_K = 2
SLOTS = 4
DEPTH = 2
W = 512
EPS = 1e-6
NEG = -1e30
TAKEN = -3e38
H1, DK1 = 4, 128
H2, DH = 8, 64
TOPK = min(256, S // 4)
FF = 4 * D
ROT = DH // 8
NF, NI = 8, 4
IN1 = 11 * W + 3 * D
QA, KA, VA, QB, KB, VB, FL, QC, KC, VC, QI, KI, WI, GL = np.cumsum(
    [0, W, W, W, W, W, W, NF, W, 128, 128, 256, 64, NI]).tolist()
IN2 = GL + 3 * D
RK, RV, DKc, DV, RQ, RG, DQ, DG, MU, MV, MG = (i * W for i in range(11))


class Tally:

    def __init__(self, eng):
        self.eng, self.reg, self.num = eng, {}, {}

    def __call__(self, sem, n=1):
        name = sem.name
        self.num[name] = self.num.get(name, 0) + n
        reg = self.reg.get(name)
        return self.num[name] if reg is None else reg + self.num[name]

    @contextmanager
    def loop(self, trips, per):
        reg, num = dict(self.reg), dict(self.num)
        with self.eng.Fori(0, trips) as i:
            for name, n in per.items():
                self.reg[name] = i * n if name not in reg else reg[name] + i * n
            yield i
            now = {k: v - num.get(k, 0) for k, v in self.num.items() if v != num.get(k, 0)}
            assert now == per, f"a trip of {self.eng.engine} waits for {now}"
        self.reg = reg
        self.num = {**num, **{k: num.get(k, 0) + trips * n for k, n in per.items()}}


def constants():
    p = np.arange(P)
    tok = np.arange(S, dtype=np.float32)
    rows, cols = (np.arange(S) // 64).astype(np.float32), (np.arange(S) % 64).astype(np.float32)

    def angles(dim):
        n = dim // 4
        inv = (np.float32(10000.0) ** (-np.arange(n, dtype=np.float32) / np.float32(n))).astype(np.float32)
        ang = np.concatenate([rows[:, None] * inv, cols[:, None] * inv], axis=-1)
        both = np.stack([np.cos(ang), np.sin(ang)], axis=1).astype(np.float32)
        return both.reshape(TT, P, 2, dim // 2).transpose(1, 0, 2, 3).reshape(P, -1)

    reach = np.stack([np.stack([S - 1 - tok, tok]), np.stack([tok + 1, S - tok])])
    reach = reach.reshape(2, 2, TT, P).transpose(3, 2, 0, 1).reshape(P, -1)
    later = (p[:, None] >= p[None, :]).astype(np.float32)
    upto = (np.arange(P)[:, None] <= np.arange(S)[None, :]).astype(np.float32)
    inv2 = (np.float32(500000.0) ** (-np.arange(0, 2 * ROT, 2, dtype=np.float32) / np.float32(2 * ROT)))
    pick = np.zeros((P, 2, P), np.float32)
    pick[0, 0], pick[64, 1] = 1, 1
    parts = dict(
        ident=np.eye(P, dtype=np.float32), rope_r=angles(DK1), rope_d=angles(DH), reach=reach,
        later=-later, every=-np.ones((P, P), np.float32), upto=-upto,
        inv2=np.tile(inv2.astype(np.float32), (P, 1)), pick=pick.reshape(P, -1))
    j = np.arange(S).reshape(TT, P).T[:, :, None]
    i = np.arange(S)[None, None, :]
    f, b = i >= j, j >= i
    dist = np.stack([np.where(f, i - j, 0), np.where(b, j - i, 0),
                     f * DK1 ** -0.5, b * DK1 ** -0.5], axis=1).astype(np.float32)
    head = np.zeros((P, NF, P), np.float32)
    for h in range(NF):
        head[h, h] = 1
    half = np.stack([np.eye(P), np.where(p[None, :] > p[:, None], NEG, 0),
                     np.where(p[:, None] >= p[None, :], NEG, 0)], axis=1).astype(np.float32)
    return parts, dist.reshape(P, -1), head.reshape(P, -1), half.reshape(P, -1)


def build(nc, g, out):
    sizes = {k: v.shape[1] for k, v in constants()[0].items()}
    place = {"at": (nc.sbuf_base + 31) // 32 * 32}

    def sb_at(name, shape, dt, offset):
        return nc.alloc_sbuf_tensor_at(name, shape, dt, offset=offset)

    def sb(name, shape, dt=F32):
        size = int(np.prod(shape[1:])) * mybir.dt.size(dt)
        at = place["at"]
        place["at"] = at + (size + 31) // 32 * 32
        place[name] = at
        return sb_at(name, shape, dt, at)

    with ExitStack() as ctx:
        def sem(name):
            return ctx.enter_context(nc.semaphore(name))

        raw = sb("raw", [P, SLOTS, SLAB_K, CH])
        whi = sb("whi", [P, SLOTS, SLAB_K, CH], F32R)
        wlo = sb("wlo", [P, SLOTS, SLAB_K, CH], F32R)
        x = sb("x", [P, TT, D])
        cx = sb("cx", [P, TT, D])
        zb = place["at"]
        z = sb("z", [P, TT, 11 * W])
        z2 = sb_at("z2", [P, TT, GL], F32, zb)
        normed = sb_at("normed", [P, TT, D], F32, zb)
        hfull = sb_at("hfull", [P, KT, S], F32, zb + 8192)
        junk = sb_at("junk", [P, D], F32, zb + 16384)
        gates = sb_at("gates", [P, TT, 3 * D], F32, zb)
        y = sb_at("y", [P, TT, D], F32, zb + 24576)
        oproj = sb_at("oproj", [P, TT, D], F32, zb + 32768)
        mtmp = sb_at("mtmp", [P, TT, CH], F32, zb + 40960)
        mod = sb_at("mod", [P, 3 * D], F32, zb)
        modb = sb_at("modb", [P, 3 * D], F32, zb + 12288)
        gpre = sb_at("gpre", [P, D], F32, zb + 24576)
        gpost = sb_at("gpost", [P, D], F32, zb + 28672)
        dist = sb_at("dist", [P, 4, TT * S], F32, zb + 32768)
        wsin = sb_at("wsin", [P, 4, P], F32, zb + 40960)
        dq = sb_at("dq", [P, 4, DH], F32, zb + 43008)
        dk = sb_at("dk", [P, 4, DH], F32, zb + 44032)
        frelu = sb_at("frelu", [P, TT, CH], F32, zb)
        fsq = sb_at("fsq", [P, TT, CH], F32, zb + 4096)
        gfin = sb_at("gfin", [P, D], F32, zb + 24576)
        hhi = sb("hhi", [P, KT, S], F32R)
        hlo = sb("hlo", [P, KT, S], F32R)
        tb = place["at"]
        tT = sb("tT", [P, 4, H1, S])
        rtmp = sb("rtmp", [P, 4, W])
        decay = sb("decay", [P, H1, TT * S])
        t2 = sb_at("t2", [P, 25, S], F32, tb)
        ohi = sb_at("ohi", [P, 3, 4, S], F32R, tb)
        olo = sb_at("olo", [P, 3, 4, S], F32R, tb + 12288)
        uhi = sb_at("uhi", [P, 4, S], F32R, tb)
        ulo = sb_at("ulo", [P, 4, S], F32R, tb + 4096)
        o = sb("o", [P, 3, TT, W])
        cb = place["at"]
        state = sb("state", [P, H1, 2, DK1])
        cdkT = sb("cdkT", [P, H1, S])
        cdv = sb("cdv", [P, TT, W])
        esel = sb_at("esel", [P, NF, P], F32, cb)
        dup = sb_at("dup", [P, TT, 3, P], F32, cb + 4096)
        work = sb_at("work", [P, 3 * P], F32, cb + 7168)
        selb = sb_at("selb", [P, 3 * P], BF16, cb + 8704)
        rt2 = sb_at("rt2", [P, 4, 10 * ROT], F32, cb + 9472)
        negc = sb_at("negc", [P, S], F32, cb + 10752)
        eb = place["at"]
        e = sb("e", [P, 2, 2, CH])
        aT = sb("aT", [P, 2, CH])
        tmp = sb_at("tmp", [P, 2, 4, 3 * P], F32, eb)
        mgate = sb("mgate", [P, D])
        modT = sb("modT", [P, 2, KT, 2])
        wsT = sb("wsT", [P, 4, P])
        cst = {k: sb("c_" + k, [P, n]) for k, n in sizes.items()}
        half = sb("half", [P, 3, P], BF16)
        ident, later, every, upto = cst["ident"], cst["later"], cst["every"], cst["upto"]
        ident16, causal16, strict16 = half[:, 0], half[:, 1], half[:, 2]
        rope_r = cst["rope_r"][:].rearrange("p (t c n) -> p t c n", t=TT, c=2)
        rope_d = cst["rope_d"][:].rearrange("p (t c n) -> p t c n", t=TT, c=2)
        pick = cst["pick"][:].rearrange("p (a m) -> p a m", a=2)
        cT = sb("cT", [P, KT, 2])
        cThi = sb("cThi", [P, KT, 2], F32R)
        cTlo = sb("cTlo", [P, KT, 2])
        eps = sb("eps", [P, 1])
        one = sb("one", [P, 1])
        ss = sb("ss", [P, 8])
        rms = sb("rms", [P, 8])
        rstd = sb("rstd", [P, 8])
        lgt = sb("lgt", [P, 6, DEPTH * 8])
        lg = sb("lg", [P, DEPTH, 2, H1])
        reachv = sb("reachv", [P, 4, 2, H1])
        lam = sb("lam", [P, 4])
        nlam = sb("nlam", [P, DEPTH])
        bs = sb("bs", [P, DEPTH, 4])
        mx = sb("mx", [P, 2, 2])
        nmx = sb("nmx", [P, 2, 2])
        sums = sb("sums", [P, 2, 2])
        rsum = sb("rsum", [P, 2, 2])
        bst = sb("bst", [P, TT, 6])
        bag = sb("bag", [P, TT, 2])
        dev = sb("dev", [P, TT])
        bfg = sb("bfg", [P, DEPTH, NF])
        gT = sb("gT", [P, 2, DEPTH, KT])
        posi = sb("posi", [P, TT], I32)
        ang = sb("ang", [P, 4, TT, ROT])
        rope_2 = sb("rope_2", [P, TT, 2, ROT])
        fg = sb("fg", [P, 3, TT, NF])
        wis = sb("wis", [P, TT, NI])
        mx8 = sb("mx8", [P, TT, 8])
        hsum = sb("hsum", [P, TT, H2])
        hrec = sb("hrec", [P, TT, H2])
        assert place["at"] <= nc.sbuf_usable_end, (place["at"], nc.sbuf_usable_end)

        G = [ctx.enter_context(nc.psum_tensor(f"G{i}", [P, CH], F32)) for i in range(4)]
        A = [ctx.enter_context(nc.psum_tensor(f"A{i}", [P, CH], F32)) for i in range(4)]

        consts_in, params_in, tokens_in = sem("consts_in"), sem("params_in"), sem("tokens_in")
        layer_in, gains_in, final_in = sem("layer_in"), sem("gains_in"), sem("final_in")
        raw_full = [sem(f"raw_full{i}") for i in range(SLOTS)]
        hi_ready, lo_ready, weights_used = sem("hi_ready"), sem("lo_ready"), sem("weights_used")
        eps_set = sem("eps_set")
        act_step, dve_step = sem("act_step"), sem("dve_step")
        silu_c, cond_split = sem("silu_c"), sem("cond_split")
        lg_exp, lg_ready, lam_dot, lam_exp = sem("lg_exp"), sem("lg_ready"), sem("lam_dot"), sem("lam_exp")
        ang_ready, sin_ready = sem("ang_ready"), sem("sin_ready")
        projected, evacuated, out_projected, out_evacuated = (sem(n) for n in (
            "projected", "evacuated", "out_projected", "out_evacuated"))
        mod_ready, mod_turned, modT_ready = sem("mod_ready"), sem("mod_turned"), sem("modT_ready")
        ws_turned, wsT_ready = sem("ws_turned"), sem("wsT_ready")
        decay_exp, decay_built, reach_arg, reach_ready = (sem(n) for n in (
            "decay_exp", "decay_built", "reach_arg", "reach_ready"))
        rms_ready, norm_ready, h_turned, h_split = (sem(n) for n in ("rms_ready", "norm_ready", "h_turned", "h_split"))
        ss_ready, x_updated = sem("ss_ready"), sem("x_updated")
        var_ready, dev_ready, topk_step = sem("var_ready"), sem("dev_ready"), sem("topk_step")
        roped, turned, turned_copied = sem("roped"), sem("turned"), sem("turned_copied")
        state_v, state_sum, state_copied = sem("state_v"), sem("state_sum"), sem("state_copied")
        ret_scores, ret_weights, ret_cross, ret_out, ret_read = (sem(n) for n in (
            "ret_scores", "ret_weights", "ret_cross", "ret_out", "ret_read"))
        diff_scores, diff_max, diff_exp, diff_mixed, diff_turned, diff_aT, diff_out, diff_read = (sem(n) for n in (
            "diff_scores", "diff_max", "diff_exp", "diff_mixed", "diff_turned", "diff_aT", "diff_out", "diff_read"))
        mlp_vn, mlp_mixed = sem("mlp_vn"), sem("mlp_mixed")
        branches_ready = sem("branches_ready")
        split_turned, split_hi, split_lo = sem("split_turned"), sem("split_hi"), sem("split_lo")
        branch_out, merged, gate_spread = sem("branch_out"), sem("merged"), sem("gate_spread")
        idx_dots, idx_relu, selected = sem("idx_dots"), sem("idx_relu"), sem("selected")
        forget_in, forget_exp, forget_log, forget_ready, cum_out, cum_copied = (sem(n) for n in (
            "forget_in", "forget_exp", "forget_log", "forget_ready", "cum_out", "cum_copied"))
        sb_scores, sb_log, sb_soft, sb_cum, sb_weights = (sem(n) for n in (
            "sb_scores", "sb_log", "sb_soft", "sb_cum", "sb_weights"))
        sm_scores, sm_max, sm_exp, sm_turned, sm_copied = (sem(n) for n in (
            "sm_scores", "sm_max", "sm_exp", "sm_turned", "sm_copied"))
        heads_out, heads_read = sem("heads_out"), sem("heads_read")
        ff_relu, ff_sq, ff_done, out_ready, out_stored = (sem(n) for n in (
            "ff_relu", "ff_sq", "ff_done", "out_ready", "out_stored"))

        PASSES = [(False, 0, True), (True, 0, True), (False, 1, False), (True, 1, True)]
        N_CONST, N_PARAM, N_LAYER, N_GAIN = len(sizes) + 1, 11, 5, 1
        slabs = DEPTH * 6 * SLOTS + 3 * (17 * SLOTS + 12 + 8) + 4 * SLOTS + DEPTH * (15 * SLOTS + 12 + 8 + 8 * 8)
        assert slabs % SLOTS == 0
        MID = [(FL, CH), (FL + CH, CH), (FL + 2 * CH, GL - FL - 2 * CH)]

        block = ctx.enter_context(nc.Block())

        @block.sync
        def _(sp):
            w = Tally(sp)
            for k in sizes:
                sp.dma_start(cst[k][:], g["k_" + k]).then_inc(consts_in, 16)
            sp.dma_start(rtmp[:, 0, 0:3 * P], g["k_half"]).then_inc(consts_in, 16)
            with nc.allow_non_contiguous_dma("small parameters, once"):
                sp.dma_start(cT[:, :, 0], g["c"][0].rearrange("(k p) -> p k", p=P)).then_inc(params_in, 16)
                sp.dma_start(cT[:, :, 1], g["c_ctx"].rearrange("(k p) -> p k", p=P)).then_inc(params_in, 16)
                sp.dma_start(lgt[:, 0, :], g["ret_decay_logit"].rearrange("l d h -> (l d h)")
                             .partition_broadcast(P)).then_inc(params_in, 16)
                sp.dma_start(dq[:].rearrange("p a n -> p (a n)"), g["diff_lambda_q"].rearrange("l a n -> (l a n)")
                             .partition_broadcast(P)).then_inc(params_in, 16)
                sp.dma_start(dk[:].rearrange("p a n -> p (a n)"), g["diff_lambda_k"].rearrange("l a n -> (l a n)")
                             .partition_broadcast(P)).then_inc(params_in, 16)
                sp.dma_start(bs[:].rearrange("p l a -> p (l a)"), g["mlp_b_s"].rearrange("l a i -> i (l a)"))\
                    .then_inc(params_in, 16)
                sp.dma_start(bfg[:].rearrange("p l n -> p (l n)"), g["b_forget_2"].rearrange("l n -> (l n)")
                             .partition_broadcast(P)).then_inc(params_in, 16)
                sp.dma_start(gT[:, 0].rearrange("p l k -> p (l k)"),
                             g["g_mix_2"].rearrange("l (k p) -> p (l k)", p=P)).then_inc(params_in, 16)
                sp.dma_start(gT[:, 1].rearrange("p l k -> p (l k)"),
                             g["g_mlp_2"].rearrange("l (k p) -> p (l k)", p=P)).then_inc(params_in, 16)
                sp.dma_start(posi[:, 0:1], g["positions_2"][0, 0:P].rearrange("(p a) -> p a", a=1)).then_inc(params_in, 16)
                sp.dma_start(posi[:, 1:2], g["positions_2"][0, P:S].rearrange("(p a) -> p a", a=1)).then_inc(params_in, 16)
            sp.dma_start(cx[:], g["ctx"][0].rearrange("(t p) d -> p t d", p=P)).then_inc(tokens_in, 16)
            sp.dma_start(x[:], g["x"][0].rearrange("(t p) d -> p t d", p=P)).then_inc(tokens_in, 16)

            def slab(mat, row, col, slot, n=CH):
                sp.wait_ge(lo_ready, w(lo_ready))
                src = mat[bass.ds(row, SLAB_K * P), bass.ds(col, n)].rearrange("(k p) n -> p k n", p=P)
                sp.dma_start(raw[:, slot, :, 0:n], src).then_inc(raw_full[slot], 16)

            def chunk(mat, row, col, n=CH):
                for s in range(SLOTS):
                    slab(mat, row + s * SLAB_K * P, col, s, n)

            def merge(wb, wo, row_b, row_o):
                for u in range(6):
                    for s in range(2):
                        slab(wb, row_b + (u % 3) * W + s * SLAB_K * P, (u // 3) * CH, 2 * (u % 2) + s)
                for n in range(D // CH):
                    chunk(wo, row_o, n * CH)

            flat = {k: g[k].rearrange("l r n -> (l r) n") for k in (
                "w_mod", "w_in", "w_out", "w_in_2", "w_out_2", "w_up_2", "w_down_2")}
            flat |= {k: g[k].rearrange("l b r n -> (l b r) n") for k in ("w_branch_out", "w_branch_2")}
            for is_x, l, full in PASSES:
                if not is_x:
                    with w.loop(3 * D // CH, {lo_ready.name: SLOTS}) as i:
                        chunk(flat["w_mod"], l * D, i * CH)
                with w.loop(IN1 // CH if full else 4, {lo_ready.name: SLOTS}) as i:
                    chunk(flat["w_in"], l * D, i * CH)
                if full:
                    merge(flat["w_branch_out"], flat["w_out"], l * 3 * W, l * D)
            with w.loop(DEPTH, {lo_ready.name: 15 * SLOTS + 12 + 8 + 8 * 8}) as l:
                with w.loop(6, {lo_ready.name: SLOTS}) as i:
                    chunk(flat["w_in_2"], l * D, i * CH)
                for col, n in MID:
                    chunk(flat["w_in_2"], l * D, col, n)
                with w.loop(6, {lo_ready.name: SLOTS}) as i:
                    chunk(flat["w_in_2"], l * D, i * CH + GL)
                merge(flat["w_branch_2"], flat["w_out_2"], l * 3 * W, l * D)
                with w.loop(FF // CH, {lo_ready.name: 2 * SLOTS}) as i:
                    chunk(flat["w_up_2"], l * D, i * CH)
                    for n in range(D // CH):
                        for s in range(2):
                            slab(flat["w_down_2"], l * FF + i * CH + s * SLAB_K * P, n * CH, 2 * n + s)
            sp.wait_ge(out_ready, w(out_ready))
            sp.dma_start(out[0].rearrange("(t p) d -> p t d", p=P), x[:]).then_inc(out_stored, 16)
            sp.wait_ge(out_stored, w(out_stored, 16))

        @block.gpsimd
        def _(pool):
            w = Tally(pool)
            pool.memset(wlo[:].bitcast(F32), 0.0).then_inc(lo_ready, SLOTS)
            with w.loop(slabs // SLOTS, {hi_ready.name: SLOTS}) as i:
                for s in range(SLOTS):
                    pool.wait_ge(hi_ready, w(hi_ready))
                    pool.tensor_tensor(wlo[:, s], raw[:, s], whi[:, s].bitcast(F32), ALU.subtract).then_inc(lo_ready, 1)

        @block.scalar
        def _(act):
            w = Tally(act)

            def link(ins):
                ins.then_inc(act_step, 1)
                act.wait_ge(act_step, w(act_step))

            def split(slot):
                act.wait_ge(raw_full[slot], w(raw_full[slot], 16))
                act.activation(whi[:, slot], raw[:, slot], ACT.Copy).then_inc(hi_ready, 1)

            def split_chunk_but_last(more=True):
                for s in range(SLOTS - 1):
                    act.wait_ge(weights_used, w(weights_used))
                    if more:
                        split(s)

            def evacuate(p, dst, func, more=True, done=evacuated):
                split_chunk_but_last(more)
                for t in range(TT):
                    act.wait_ge(projected, w(projected))
                    act.activation(dst[t], G[2 * p + t][:, 0:dst[t].shape[-1]], func).then_inc(done, 1)
                if more:
                    split(SLOTS - 1)

            def pair_counts(n_chunks):
                d = {weights_used.name: 3 * n_chunks, projected.name: TT * n_chunks}
                return d | {raw_full[s].name: 16 * n_chunks for s in range(SLOTS)}

            def columns(dst, c):
                return [dst[:, t, bass.ds(c, CH)] for t in range(TT)]

            def norm(src):
                for t in range(TT):
                    ins = act.activation(junk[:], src[:, t], ACT.Square, accum_out=ss[:, t:t + 1])
                    link(ins)
                act.activation(rms[:, 0:TT], ss[:, 0:TT], ACT.Sqrt, bias=eps[:], scale=1.0 / D).then_inc(rms_ready, 1)

            def copy_turned(dsts, scales):
                for n, (dst, scale) in enumerate(zip(dsts, scales)):
                    act.wait_ge(turned, w(turned))
                    act.activation(dst, A[n % 4][:, 0:dst.shape[-1]], ACT.Copy, scale=scale).then_inc(turned_copied, 1)

            def split_high(dsts):
                for n, dst in enumerate(dsts):
                    act.wait_ge(split_turned, w(split_turned))
                    act.activation(dst, A[n % 4][:], ACT.Copy).then_inc(split_hi, 1)

            def two_kt(buf, n=KT):
                return [buf[:, 2 * q:2 * q + 2, :].rearrange("p k s -> p (k s)") for q in range(n // 2)]

            def merge(more, in_first):
                split_high([ap for b in range(3) for ap in two_kt(ohi[:, b], 4)])
                for u in range(6):
                    act.wait_ge(weights_used, w(weights_used))
                    split(2 * (u % 2))
                    act.wait_ge(branch_out, w(branch_out, TT))
                    split(2 * (u % 2) + 1)
                split_high(two_kt(hhi))
                for n in range(D // CH):
                    if in_first:
                        evacuate(n, columns(oproj, n * CH), ACT.Copy, more or n == 0, out_evacuated)
                    else:
                        split_chunk_but_last()
                        act.wait_ge(out_projected, w(out_projected, TT))
                        split(SLOTS - 1)

            act.wait_ge(eps_set, w(eps_set, 2))
            act.wait_ge(params_in, w(params_in, 16 * N_PARAM))
            act.activation(cT[:].rearrange("p k a -> p (k a)"), cT[:].rearrange("p k a -> p (k a)"), ACT.Silu)\
               .then_inc(silu_c, 1)
            act.wait_ge(lg_ready, w(lg_ready))
            act.activation(lgt[:, 2], lgt[:, 1], ACT.Exp, scale=-1.0).then_inc(lg_exp, 1)
            act.wait_ge(lam_dot, w(lam_dot))
            act.activation(lam[:], lam[:], ACT.Exp).then_inc(lam_exp, 1)
            act.wait_ge(ang_ready, w(ang_ready))
            act.activation(rope_2[:, :, 0, :], ang[:, 3], ACT.Sin)
            act.activation(rope_2[:, :, 1, :], ang[:, 2], ACT.Sin).then_inc(sin_ready, 1)
            for s in range(SLOTS):
                split(s)
            act.wait_ge(tokens_in, w(tokens_in, 32))
            act.wait_ge(lg_ready, w(lg_ready))

            for n, (is_x, l, full) in enumerate(PASSES):
                if not is_x:
                    act.dma_start(modb[:], g["b_mod"][l].partition_broadcast(P)).then_inc(layer_in, 16)
                    act.dma_start(gpre[:], g["g_pre"][l].partition_broadcast(P)).then_inc(layer_in, 16)
                    act.dma_start(gpost[:], g["g_post"][l].partition_broadcast(P)).then_inc(layer_in, 16)
                    act.dma_start(dist[:].rearrange("p a n -> p (a n)"), g["k_dist"]).then_inc(layer_in, 16)
                    act.dma_start(wsin[:], g["mlp_w_s"][l].rearrange("a i j -> i a j")).then_inc(layer_in, 16)
                    per = {weights_used.name: 6, projected.name: 2} | {raw_full[s].name: 32 for s in range(SLOTS)}
                    with w.loop(3, per) as i:
                        for p in range(2):
                            split_chunk_but_last()
                            act.wait_ge(projected, w(projected))
                            act.activation(mod[:, bass.ds(i * (2 * CH) + p * CH, CH)], G[p][:], ACT.Copy).then_inc(evacuated, 1)
                            split(SLOTS - 1)
                    act.wait_ge(layer_in, w(layer_in, 16 * N_LAYER))
                    for h in range(H1):
                        if h >= 2:
                            act.wait_ge(decay_built, w(decay_built))
                        act.activation(e[:, h % 2, 0], dist[:, 0], ACT.Exp, scale=lg[:, l, 0, h:h + 1])
                        act.activation(e[:, h % 2, 1], dist[:, 1], ACT.Exp, scale=lg[:, l, 1, h:h + 1]).then_inc(decay_exp, 1)
                    act.wait_ge(decay_built, w(decay_built, 2))
                    act.wait_ge(reach_arg, w(reach_arg))
                    act.activation(reachv[:].rearrange("p a d h -> p (a d h)"), reachv[:].rearrange("p a d h -> p (a d h)"),
                                   ACT.Exp).then_inc(reach_ready, 1)
                    act.wait_ge(ws_turned, w(ws_turned))
                    act.activation(wsT[:].rearrange("p a i -> p (a i)"), A[0][:], ACT.Copy).then_inc(wsT_ready, 1)
                    for q in range(4):
                        act.wait_ge(mod_turned, w(mod_turned))
                        act.activation(modT[:, q // 2, 4 * (q % 2):4 * (q % 2) + 4, :],
                                       A[q][:].rearrange("p (k m) -> p k m", k=4)[:, :, 0::64], ACT.Copy).then_inc(modT_ready, 1)
                norm(x if is_x else cx)
                with w.loop(2, pair_counts(2)) as i:
                    for p in range(2):
                        evacuate(p, columns(z, i * (2 * W) + p * W), ACT.Copy)
                if full:
                    with w.loop(2, pair_counts(2)) as i:
                        evacuate(0, columns(z, i * (2 * W) + RQ), ACT.Copy)
                        evacuate(1, columns(z, i * (2 * W) + RG), ACT.Silu)
                    evacuate(0, columns(z, MU), ACT.Copy)
                    evacuate(1, columns(z, MV), ACT.Copy)
                    evacuate(0, columns(z, MG), ACT.Silu)
                if full:
                    copy_turned([tT[:, a, 2 * b:2 * b + 2].rearrange("p h s -> p (h s)") for a in range(4) for b in range(2)],
                                [1.0] * 8)
                else:
                    copy_turned([cdkT[:, 2 * b:2 * b + 2].rearrange("p h s -> p (h s)") for b in range(2)], [1.0] * 2)
                if not is_x:
                    if full:
                        act.wait_ge(turned_copied, w(turned_copied, 8))
                        act.activation(cdkT[:].rearrange("p h s -> p (h s)"), tT[:, 2].rearrange("p h s -> p (h s)"), ACT.Copy)
                    for t in range(TT):
                        act.activation(cdv[:, t], z[:, t, DV:DV + W], ACT.Copy).then_inc(turned_copied, 1)
                    for h in range(H1):
                        act.wait_ge(state_sum, w(state_sum))
                        act.activation(state[:, h].rearrange("p d n -> p (d n)"), A[h % 4][:, 0:2 * DK1], ACT.Copy,
                                       scale=DK1 ** -0.5).then_inc(state_copied, 1)
                if not full:
                    continue
                m = H1 * TT
                nk = 2 * S if is_x else S
                for i in range(m + 2):
                    if i >= 2:
                        h, t = divmod(i - 2, TT)
                        act.wait_ge(diff_out, w(diff_out))
                        act.activation(o[:, 2, t, h * P:(h + 1) * P], A[2 * (i % 2) + 1][:, 0:P], ACT.Copy).then_inc(diff_read, 1)
                    if i < m:
                        act.wait_ge(diff_max, w(diff_max))
                        for b in range(2):
                            ins = act.activation(e[:, i % 2, b, 0:nk], A[2 * (i % 2) + b][:, 0:nk], ACT.Exp, scale=DH ** -0.5,
                                                 bias=nmx[:, i % 2, b:b + 1], accum_out=sums[:, i % 2, b:b + 1])
                        ins.then_inc(diff_exp, 1)
                    if 1 <= i <= m:
                        j = i - 1
                        act.wait_ge(diff_turned, w(diff_turned))
                        act.activation(aT[:, j % 2, 0:nk], A[2 * (j % 2)][:, 0:nk], ACT.Copy).then_inc(diff_aT, 1)
                act.wait_ge(ss_ready, w(ss_ready))
                act.activation(rms[:, 0:8], ss[:, 0:8], ACT.Sqrt, bias=eps[:], scale=1.0 / P).then_inc(rms_ready, 1)
                act.wait_ge(ss_ready, w(ss_ready))
                act.activation(rms[:, 0:8], ss[:, 0:8], ACT.Sqrt, bias=eps[:], scale=1.0 / P).then_inc(rms_ready, 1)
                act.wait_ge(var_ready, w(var_ready))
                act.activation(dev[:], bag[:, :, 1], ACT.Sqrt, bias=eps[:]).then_inc(dev_ready, 1)
                act.wait_ge(branches_ready, w(branches_ready, 3))
                with w.loop(3, pair_counts(2)) as i:
                    for p in range(2):
                        evacuate(p, columns(gates, i * (2 * CH) + p * CH), ACT.Sigmoid)
                last = n == len(PASSES) - 1
                merge(not last, True)
                act.wait_ge(out_evacuated, w(out_evacuated, 2 * TT))
                norm(oproj)
                act.wait_ge(x_updated, w(x_updated))
            act.dma_start(esel[:].rearrange("p a n -> p (a n)"), g["k_head"]).then_inc(gains_in, 16)

            def layer(l):
                for s in range(SLOTS):
                    split(s)
                norm(x)
                with w.loop(3, pair_counts(2)) as i:
                    for p in range(2):
                        evacuate(p, columns(z2, i * (2 * CH) + p * CH), ACT.Copy)
                for n, (col, width) in enumerate(MID):
                    evacuate(n % 2, [z2[:, t, col:col + width] for t in range(TT)], ACT.Copy)
                copy_turned([t2[:, 2 * n:min(2 * n + 2, 25)].rearrange("p b s -> p (b s)") for n in range(13)],
                            [DH ** -0.5] * 2 + [1.0] * 2 + [DH ** -0.5] * 2 + [1.0] * 2 + [DH ** -0.5] * 2 + [1.0] * 3)
                for h in range(NI):
                    act.wait_ge(idx_dots, w(idx_dots))
                    act.activation(tmp[:, h % 2, h // 2], A[h][:, 0:3 * P], ACT.Relu).then_inc(idx_relu, 1)
                act.wait_ge(forget_in, w(forget_in))
                act.activation(fg[:, 1], fg[:, 1], ACT.Exp, scale=-1.0).then_inc(forget_exp, 1)
                act.wait_ge(forget_exp, w(forget_exp))
                act.activation(fg[:, 1], fg[:, 1], ACT.Ln, bias=one[:]).then_inc(forget_log, 1)
                act.wait_ge(cum_out, w(cum_out))
                act.activation(negc[0:NF, :], A[0][0:NF, 0:S], ACT.Copy).then_inc(cum_copied, 1)
                act.wait_ge(selected, w(selected))
                for i in range(H2 + 1):
                    if i < H2:
                        act.wait_ge(sb_scores, w(sb_scores))
                        link(act.activation(tmp[:, i % 2, 0], A[i % 2][:, 0:3 * P], ACT.Abs))
                        link(act.activation(tmp[:, i % 2, 0], tmp[:, i % 2, 0], ACT.Exp, scale=-1.0))
                        act.activation(tmp[:, i % 2, 1], tmp[:, i % 2, 0], ACT.Ln, bias=one[:]).then_inc(sb_log, 1)
                    if i >= 1:
                        j = i - 1
                        act.wait_ge(sb_cum, w(sb_cum))
                        act.activation(tmp[:, j % 2, 3], A[j % 2][:, 0:3 * P], ACT.Exp).then_inc(sb_weights, 1)
                for grp in range(2):
                    for i in range(H2 + 1):
                        if i < H2:
                            act.wait_ge(sm_max, w(sm_max))
                            act.activation(tmp[:, i % 2, 0, 0:P], A[i % 2][:, 0:P], ACT.Exp, bias=nmx[:, i % 2, 0:1],
                                           accum_out=hsum[:, 0, i:i + 1])
                            act.activation(tmp[:, i % 2, 0, P:3 * P], A[i % 2][:, P:3 * P], ACT.Exp, bias=nmx[:, i % 2, 1:2],
                                           accum_out=hsum[:, 1, i:i + 1]).then_inc(sm_exp, 1)
                        if i >= 1:
                            j = i - 1
                            act.wait_ge(sm_turned, w(sm_turned))
                            act.activation(tmp[:, j % 2, 1], A[j % 2][:, 0:3 * P], ACT.Copy).then_inc(sm_copied, 1)
                    if grp == 0:
                        act.wait_ge(heads_read, w(heads_read, 2))
                act.wait_ge(heads_read, w(heads_read))
                with w.loop(3, pair_counts(2)) as i:
                    for p in range(2):
                        evacuate(p, columns(gates, i * (2 * CH) + p * CH), ACT.Sigmoid)
                merge(True, False)
                act.wait_ge(x_updated, w(x_updated))
                norm(x)

                def up_down(more):
                    split_chunk_but_last()
                    for t in range(TT):
                        act.wait_ge(projected, w(projected))
                        act.activation(frelu[:, t], G[t][:], ACT.Relu).then_inc(ff_relu, 1)
                    split(SLOTS - 1)
                    split_high(two_kt(uhi, 4))
                    for s in range(SLOTS):
                        if more or s < SLOTS - 1:
                            act.wait_ge(weights_used, w(weights_used))
                        if more:
                            split(s)

                per = {weights_used.name: 7, projected.name: TT, split_turned.name: 2}
                per |= {raw_full[s].name: 32 for s in range(SLOTS)}
                with w.loop(FF // CH - 1, per) as i:
                    up_down(True)
                up_down(False)
                act.wait_ge(x_updated, w(x_updated))

            with w.loop(DEPTH, LAYER_ACT) as l:
                layer(l)
            act.dma_start(gfin[:], g["g_final_2"].partition_broadcast(P)).then_inc(final_in, 16)
            norm(x)

        @block.vector
        def _(dve):
            w = Tally(dve)

            def link(ins):
                ins.then_inc(dve_step, 1)
                dve.wait_ge(dve_step, w(dve_step))

            def norm_and_split(src, scale, shift):
                dve.wait_ge(rms_ready, w(rms_ready))
                link(dve.reciprocal(rstd[:, 0:TT], rms[:, 0:TT]))
                for t in range(TT):
                    dve.tensor_scalar(normed[:, t], src[:, t], rstd[:, t:t + 1], None, ALU.mult).then_inc(norm_ready, 1)
                for q in range(4):
                    dve.wait_ge(h_turned, w(h_turned))
                    for k in range(2 * q, 2 * q + 2):
                        part = A[q][:, (k % 2) * S:(k % 2 + 1) * S]
                        if shift is None:
                            ins = dve.tensor_scalar(hfull[:, k], part, scale(k), None, ALU.mult)
                        else:
                            ins = dve.tensor_scalar(hfull[:, k], part, scale(k), shift(k), ALU.mult, ALU.add)
                    link(ins)
                    both = slice(2 * q, 2 * q + 2)
                    link(dve.tensor_copy(hhi[:, both], hfull[:, both]))
                    dve.tensor_tensor(hlo[:, both], hfull[:, both], hhi[:, both].bitcast(F32), ALU.subtract)\
                       .then_inc(h_split, 1)

            def split_low(dst_hi, dst_lo):
                for n, (hi, lo) in enumerate(zip(dst_hi, dst_lo)):
                    dve.wait_ge(split_hi, w(split_hi))
                    dve.tensor_tensor(lo, A[n % 4][:], hi.bitcast(F32), ALU.subtract).then_inc(split_lo, 1)

            def two_kt(buf, n=KT):
                return [buf[:, 2 * q:2 * q + 2, :].rearrange("p k s -> p (k s)") for q in range(n // 2)]

            def rotate(x1, x2, cos, sin, temps):
                a, b, c, d = temps
                dve.tensor_tensor(a, x1, cos, ALU.mult)
                dve.tensor_tensor(b, x2, sin, ALU.mult)
                dve.tensor_tensor(c, x1, sin, ALU.mult)
                link(dve.tensor_tensor(d, x2, cos, ALU.mult))
                dve.tensor_tensor(x1, a, b, ALU.subtract)
                return dve.tensor_tensor(x2, c, d, ALU.add)

            def merge():
                split_low([ap for b in range(3) for ap in two_kt(ohi[:, b], 4)],
                          [ap for b in range(3) for ap in two_kt(olo[:, b], 4)])
                dve.wait_ge(evacuated, w(evacuated, 2 * TT + 6 * TT))
                for u in range(6):
                    n, b = divmod(u, 3)
                    for t in range(TT):
                        dve.wait_ge(branch_out, w(branch_out))
                        part, gate = y[:, t, n * CH:(n + 1) * CH], gates[:, t, b * D + n * CH:b * D + (n + 1) * CH]
                        bank = G[2 * (u % 2) + t]
                        if b == 0:
                            dve.tensor_tensor(part, bank[:], gate, ALU.mult).then_inc(merged, 1)
                        else:
                            link(dve.tensor_tensor(e[:, u % 2, t], bank[:], gate, ALU.mult))
                            dve.tensor_tensor(part, part, e[:, u % 2, t], ALU.add).then_inc(merged, 1)
                split_low(two_kt(hhi), two_kt(hlo))

            dve.memset(eps[:], EPS).then_inc(eps_set, 1)
            dve.memset(one[:], 1.0).then_inc(eps_set, 1)
            dve.wait_ge(params_in, w(params_in, 16 * N_PARAM))
            dve.wait_ge(consts_in, w(consts_in, 16 * N_CONST))
            dve.tensor_copy(half[:].rearrange("p a n -> p (a n)"), rtmp[:, 0, 0:3 * P])
            dve.scalar_tensor_tensor(lgt[:, 1], lgt[:, 0], -1.0, lgt[:, 0], ALU.mult, ALU.max).then_inc(lg_ready, 1)
            link(dve.tensor_tensor(dq[:], dq[:], dk[:], ALU.mult))
            dve.tensor_reduce(lam[:], dq[:], AX.X, ALU.add).then_inc(lam_dot, 1)
            dve.wait_ge(lg_exp, w(lg_exp))
            u, den, t1, t2_, acc = lgt[:, 2], lgt[:, 3], lgt[:, 4], lgt[:, 5], lgt[:, 3]
            link(dve.tensor_scalar(den, u, 2.0, None, ALU.add))
            link(dve.reciprocal(den, den))
            link(dve.tensor_tensor(t1, u, den, ALU.mult))
            link(dve.tensor_tensor(t2_, t1, t1, ALU.mult))
            link(dve.tensor_scalar(acc, t2_, 2.0 / 19, None, ALU.mult))
            for n in range(17, 1, -2):
                link(dve.scalar_tensor_tensor(acc, acc, 2.0 / n, t2_, ALU.add, ALU.mult))
            link(dve.scalar_tensor_tensor(acc, acc, 2.0, t1, ALU.add, ALU.mult))
            link(dve.tensor_scalar(t1, lgt[:, 0], 0.0, None, ALU.min))
            dve.tensor_tensor(lg[:].rearrange("p l d h -> p (l d h)"), t1, acc, ALU.subtract).then_inc(lg_ready, 1)
            dve.wait_ge(lam_exp, w(lam_exp))
            for l in range(DEPTH):
                start = 0.8 - 0.6 * math.exp(-0.3 * l)
                link(dve.tensor_tensor(nlam[:, l:l + 1], lam[:, 2 * l + 1:2 * l + 2], lam[:, 2 * l:2 * l + 1], ALU.subtract))
                link(dve.tensor_scalar(nlam[:, l:l + 1], nlam[:, l:l + 1], -start, None, ALU.add))
            dve.wait_ge(silu_c, w(silu_c))
            link(dve.tensor_copy(cThi[:], cT[:]))
            link(dve.tensor_tensor(cTlo[:], cT[:], cThi[:].bitcast(F32), ALU.subtract))
            pos = ang[:, 0, :, 0]
            link(dve.tensor_copy(pos, posi[:]))
            for t in range(TT):
                ins = dve.tensor_scalar(ang[:, 1, t], cst["inv2"][:], ang[:, 0, t, 0:1], None, ALU.mult)
            link(ins)
            big = 1.5 * 2.0 ** 23
            link(dve.tensor_scalar(ang[:, 3], ang[:, 1], 1.0 / (2 * math.pi), big, ALU.mult, ALU.add))
            link(dve.tensor_scalar(ang[:, 3], ang[:, 3], big, None, ALU.subtract))
            turn = [6.28125, 0.00193500518798828125, 2 * math.pi - 6.28125 - 0.00193500518798828125]
            src = ang[:, 1]
            for c in turn:
                link(dve.scalar_tensor_tensor(ang[:, 2], ang[:, 3], -c, src, ALU.mult, ALU.add))
                src = ang[:, 2]
            link(dve.tensor_scalar(ang[:, 2], ang[:, 2], math.pi, -math.pi, ALU.min, ALU.max))
            link(dve.scalar_tensor_tensor(ang[:, 3], ang[:, 2], -1.0, ang[:, 2], ALU.mult, ALU.max))
            dve.tensor_scalar(ang[:, 3], ang[:, 3], -1.0, math.pi / 2, ALU.mult, ALU.add).then_inc(ang_ready, 1)
            dve.wait_ge(tokens_in, w(tokens_in, 32))

            for n, (is_x, l, full) in enumerate(PASSES):
                src = x if is_x else cx
                if not is_x:
                    for a in range(2):
                        cols = slice(64 * a, 64 * a + 64)
                        dve.tensor_copy(hhi[:, :, cols], cThi[:, :, a:a + 1].bitcast(F32).to_broadcast([P, KT, 64]))
                        ins = dve.tensor_copy(hlo[:, :, cols], cTlo[:, :, a:a + 1].to_broadcast([P, KT, 64]))
                    ins.then_inc(cond_split, 1)
                    dve.wait_ge(layer_in, w(layer_in, 16 * N_LAYER))
                    dve.wait_ge(evacuated, w(evacuated, 2 + 6))
                    link(dve.tensor_tensor(mod[:], mod[:], modb[:], ALU.add))
                    dve.tensor_tensor(mgate[:], mod[:, 2 * D:], gpost[:], ALU.mult)
                    dve.scalar_tensor_tensor(mod[:, D:2 * D], mod[:, D:2 * D], 1.0, gpre[:], ALU.add, ALU.mult)\
                       .then_inc(mod_ready, 1)
                    for h in range(H1):
                        dve.wait_ge(decay_exp, w(decay_exp))
                        dve.tensor_tensor(e[:, h % 2, 0], e[:, h % 2, 0], dist[:, 2], ALU.mult)
                        link(dve.tensor_tensor(e[:, h % 2, 1], e[:, h % 2, 1], dist[:, 3], ALU.mult))
                        dve.tensor_tensor(decay[:, h], e[:, h % 2, 0], e[:, h % 2, 1], ALU.add).then_inc(decay_built, 1)
                    for a in range(4):
                        rc = cst["reach"][:].rearrange("p (a d) -> p a d", a=4)[:, a, :].unsqueeze(2).to_broadcast([P, 2, H1])
                        ins = dve.tensor_tensor(reachv[:, a], lg[:, l], rc, ALU.mult)
                    ins.then_inc(reach_arg, 1)
                    dve.wait_ge(modT_ready, w(modT_ready, 4))
                a = 0 if is_x else 1
                norm_and_split(src, lambda k: modT[:, 1, k, a:a + 1], lambda k: modT[:, 0, k, a:a + 1])
                dve.wait_ge(evacuated, w(evacuated, 2 * TT + (11 if full else 4) * TT))
                if is_x:
                    for col in (RK, RQ):
                        v = z[:, :, col:col + W].rearrange("p t (h c n) -> p t h c n", h=H1, c=2)
                        for t in range(TT):
                            cos, sin = (rope_r[:, t, c].unsqueeze(1).to_broadcast([P, H1, DK1 // 2]) for c in range(2))
                            temps = [rtmp[:, q, 0:W // 2].rearrange("p (h n) -> p h n", h=H1) for q in range(4)]
                            link(rotate(v[:, t, :, 0], v[:, t, :, 1], cos, sin, temps))
                    for col in (DKc, DQ):
                        v = z[:, :, col:col + W].rearrange("p t (h c n) -> p t h c n", h=2 * H1, c=2)
                        for t in range(TT):
                            cos, sin = (rope_d[:, t, c].unsqueeze(1).to_broadcast([P, 2 * H1, DH // 2]) for c in range(2))
                            temps = [rtmp[:, q, 0:W // 2].rearrange("p (h n) -> p h n", h=2 * H1) for q in range(4)]
                            ins = rotate(v[:, t, :, 0], v[:, t, :, 1], cos, sin, temps)
                            if (col, t) == (DQ, TT - 1):
                                ins.then_inc(roped, 1)
                            else:
                                link(ins)
                else:
                    dve.wait_ge(reach_ready, w(reach_ready))
                    for h in range(H1):
                        if h >= 2:
                            dve.wait_ge(state_sum, w(state_sum))
                        for t in range(TT):
                            for d in range(2):
                                ins = dve.tensor_scalar(e[:, h % 2, t, d * DK1:(d + 1) * DK1],
                                                        z[:, t, RV + h * DK1:RV + (h + 1) * DK1],
                                                        reachv[:, 2 * t, d, h:h + 1], None, ALU.mult)
                        ins.then_inc(state_v, 1)
                    dve.wait_ge(state_sum, w(state_sum, 2))
                if not full:
                    continue
                for i in range(H1 + 1):
                    if i < H1:
                        dve.wait_ge(ret_scores, w(ret_scores))
                        dve.tensor_tensor(e[:, i % 2, 0], A[i % 2][:], decay[:, i], ALU.mult).then_inc(ret_weights, 1)
                    if i >= 1:
                        h = i - 1
                        if is_x:
                            dve.wait_ge(ret_cross, w(ret_cross))
                            cross = A[2 + h % 2][:].rearrange("p (t d n) -> p t d n", t=TT, d=2)
                            for t in range(TT):
                                ins = dve.tensor_scalar(e[:, h % 2, 1, t * P:(t + 1) * P], cross[:, t, 0],
                                                        reachv[:, 2 * t + 1, 0, h:h + 1], None, ALU.mult)
                            link(ins)
                            for t in range(TT):
                                part = e[:, h % 2, 1, t * P:(t + 1) * P]
                                ins = dve.scalar_tensor_tensor(part, cross[:, t, 1], reachv[:, 2 * t + 1, 1, h:h + 1], part,
                                                               ALU.mult, ALU.add)
                            link(ins)
                        dve.wait_ge(ret_out, w(ret_out))
                        inner = A[h % 2][:, 0:TT * P].rearrange("p (t n) -> p t n", t=TT)
                        res = o[:, 0, :, h * P:(h + 1) * P]
                        if is_x:
                            part = e[:, h % 2, 1, 0:TT * P].rearrange("p (t n) -> p t n", t=TT)
                            dve.tensor_tensor(res, inner, part, ALU.add).then_inc(ret_read, 1)
                        else:
                            dve.tensor_copy(res, inner).then_inc(ret_read, 1)
                for t in range(TT):
                    link(dve.bn_stats(bst[:, t], z[:, t, MV:MV + W]))
                    ins = dve.bn_aggr(bag[:, t], bst[:, t])
                ins.then_inc(var_ready, 1)
                m = H1 * TT
                nk = 2 * S if is_x else S

                def mix(i):
                    dve.wait_ge(diff_exp, w(diff_exp))
                    link(dve.reciprocal(rsum[:, i % 2], sums[:, i % 2]))
                    dve.tensor_scalar(e[:, i % 2, 0, 0:nk], e[:, i % 2, 0, 0:nk], rsum[:, i % 2, 0:1], None, ALU.mult)
                    link(dve.tensor_tensor(rsum[:, i % 2, 1:2], rsum[:, i % 2, 1:2], nlam[:, l:l + 1], ALU.mult))
                    dve.scalar_tensor_tensor(e[:, i % 2, 0, 0:nk], e[:, i % 2, 1, 0:nk], rsum[:, i % 2, 1:2], e[:, i % 2, 0, 0:nk],
                                             ALU.mult, ALU.add).then_inc(diff_mixed, 1)

                for i in range(m + 1):
                    if i < m:
                        dve.wait_ge(diff_scores, w(diff_scores))
                        for b in range(2):
                            ins = dve.reduce_max(mx[:, i % 2, b:b + 1], A[2 * (i % 2) + b][:, 0:nk], AX.X)
                        link(ins)
                        dve.tensor_scalar(nmx[:, i % 2], mx[:, i % 2], -DH ** -0.5, None, ALU.mult).then_inc(diff_max, 1)
                    if i >= 1:
                        mix(i - 1)
                dve.wait_ge(diff_read, w(diff_read, m))
                for b, gate in ((0, RG), (2, DG)):
                    ob = o[:, b].rearrange("p t (h n) -> p (t h) n", h=H1)
                    sq = rtmp[:].rearrange("p a n -> p (a n)")[:, 0:TT * W].rearrange("p (q n) -> p q n", q=TT * H1)
                    link(dve.tensor_tensor(sq, ob, ob, ALU.mult))
                    dve.tensor_reduce(ss[:, 0:8], sq, AX.X, ALU.add).then_inc(ss_ready, 1)
                    dve.wait_ge(rms_ready, w(rms_ready))
                    link(dve.reciprocal(rstd[:], rms[:]))
                    if b == 2:
                        link(dve.tensor_scalar(rstd[:], rstd[:], 1.0 - (0.8 - 0.6 * math.exp(-0.3 * l)), None, ALU.mult))
                    link(dve.tensor_tensor(ob, ob, rstd[:].unsqueeze(2).to_broadcast([P, 8, P]), ALU.mult))
                    dve.tensor_tensor(o[:, b], o[:, b], z[:, :, gate:gate + W], ALU.mult).then_inc(branches_ready, 1)
                dve.wait_ge(dev_ready, w(dev_ready))
                link(dve.reciprocal(rstd[:, 0:TT], dev[:]))
                for t in range(TT):
                    dve.tensor_scalar(z[:, t, MV:MV + W], z[:, t, MV:MV + W], bag[:, t, 0:1], rstd[:, t:t + 1],
                                      ALU.subtract, ALU.mult).then_inc(mlp_vn, 1)
                for t in range(TT):
                    dve.wait_ge(mlp_mixed, w(mlp_mixed))
                    for b in range(4):
                        cols = slice(MU + b * P, MU + (b + 1) * P)
                        ins = dve.scalar_tensor_tensor(o[:, 1, t, b * P:(b + 1) * P], A[t][:, b * P:(b + 1) * P],
                                                       bs[:, l, b:b + 1], z[:, t, cols], ALU.add, ALU.mult)
                    link(ins)
                dve.tensor_tensor(o[:, 1], o[:, 1], z[:, :, MG:MG + W], ALU.mult).then_inc(branches_ready, 1)
                merge()
                dve.wait_ge(out_evacuated, w(out_evacuated, 2 * TT))
                dve.wait_ge(rms_ready, w(rms_ready))
                link(dve.reciprocal(rstd[:, 0:TT], rms[:, 0:TT]))
                for c in range(D // CH):
                    dve.wait_ge(gate_spread, w(gate_spread))
                    for t in range(TT):
                        cols = slice(c * CH, (c + 1) * CH)
                        link(dve.scalar_tensor_tensor(mtmp[:, t], oproj[:, t, cols], rstd[:, t:t + 1], A[c][:],
                                                      ALU.mult, ALU.mult))
                        ins = dve.tensor_tensor(src[:, t, cols], src[:, t, cols], mtmp[:, t], ALU.add)
                    if c == 0:
                        link(ins)
                ins.then_inc(x_updated, 1)
            dve.wait_ge(sin_ready, w(sin_ready))

            def layer(l):
                norm_and_split(x, lambda k: gT[:, 0, bass.ds(l, 1), k], None)
                dve.wait_ge(evacuated, w(evacuated, 2 * TT + 9 * TT))
                for t in range(TT):
                    cos, sin = (rope_2[:, t, c] for c in range(2))
                    for col, nh in ((QC, 10), (QI, 5)):
                        v = z2[:, t, col:col + nh * DH].rearrange("p (h n) -> p h n", n=DH)
                        temps = [rt2[:, q, 0:nh * ROT].rearrange("p (h n) -> p h n", h=nh) for q in range(4)]
                        link(rotate(v[:, :, 0:ROT], v[:, :, ROT:2 * ROT], cos.unsqueeze(1).to_broadcast([P, nh, ROT]),
                                    sin.unsqueeze(1).to_broadcast([P, nh, ROT]), temps))
                for t in range(TT):
                    for c in range(2):
                        dve.tensor_copy(dup[:, t, 0:2, c * DH:(c + 1) * DH],
                                        z2[:, t, KC:KC + 2 * DH].rearrange("p (g n) -> p g n", g=2))
                        ins = dve.tensor_copy(dup[:, t, 2, c * DH:(c + 1) * DH], z2[:, t, KI:KI + DH])
                ins.then_inc(roped, 1)
                for t in range(TT):
                    ins = dve.tensor_tensor(fg[:, 0, t], z2[:, t, FL:FL + NF], bfg[:, bass.ds(l, 1), :].rearrange("p a n -> p (a n)"), ALU.add)
                link(ins)
                dve.scalar_tensor_tensor(fg[:, 1], fg[:, 0], -1.0, fg[:, 0], ALU.mult, ALU.max).then_inc(forget_in, 1)
                link(dve.tensor_scalar(fg[:, 2], fg[:, 0], 0.0, None, ALU.min))
                dve.wait_ge(forget_log, w(forget_log))
                dve.tensor_tensor(fg[:, 2], fg[:, 2], fg[:, 1], ALU.subtract).then_inc(forget_ready, 1)
                link(dve.tensor_scalar(wis[:], z2[:, :, WI:WI + NI], NI ** -0.5 * DH ** -0.5, None, ALU.mult))
                tiles = [slice(0, P), slice(P, 3 * P)]
                for h in range(NI):
                    dve.wait_ge(idx_relu, w(idx_relu))
                    for t in range(TT):
                        r = tmp[:, h % 2, h // 2, tiles[t]]
                        if h == 0:
                            ins = dve.tensor_scalar(work[:, tiles[t]], r, wis[:, t, h:h + 1], 0.0, ALU.mult, ALU.add)
                        else:
                            ins = dve.scalar_tensor_tensor(work[:, tiles[t]], r, wis[:, t, h:h + 1], work[:, tiles[t]],
                                                           ALU.mult, ALU.add)
                    link(ins)
                dve.tensor_tensor(work[:, 0:P], work[:, 0:P], causal16, ALU.add)
                link(dve.tensor_tensor(work[:, 2 * P:], work[:, 2 * P:], causal16, ALU.add))
                for r in range(TOPK // 8):
                    dve.sem_inc(topk_step, 1)
                    for t in range(TT):
                        ins = dve.max(mx8[:, t], work[:, tiles[t]])
                    link(ins)
                    dve.sem_inc(topk_step, 1)
                    for t in range(TT):
                        ins = dve.match_replace(work[:, tiles[t]], mx8[:, t], work[:, tiles[t]], TAKEN)
                    link(ins)
                dve.tensor_scalar(selb[:], work[:], TAKEN, NEG, ALU.not_equal, ALU.mult).then_inc(selected, 1)
                for i in range(H2):
                    dve.wait_ge(sb_log, w(sb_log))
                    dve.scalar_tensor_tensor(tmp[:, i % 2, 2], A[i % 2][:, 0:3 * P], 0.0, tmp[:, i % 2, 1],
                                             ALU.max, ALU.add).then_inc(sb_soft, 1)
                dve.wait_ge(heads_out, w(heads_out))
                for t in range(TT):
                    ins = dve.tensor_copy(o[:, 0, t], A[2 + t][:])
                ins.then_inc(heads_read, 1)
                for grp in range(2):
                    for i in range(H2):
                        dve.wait_ge(sm_scores, w(sm_scores))
                        dve.reduce_max(mx[:, i % 2, 0:1], A[i % 2][:, 0:P], AX.X)
                        link(dve.reduce_max(mx[:, i % 2, 1:2], A[i % 2][:, P:3 * P], AX.X))
                        dve.tensor_scalar(nmx[:, i % 2], mx[:, i % 2], -1.0, None, ALU.mult).then_inc(sm_max, 1)
                    dve.wait_ge(heads_out, w(heads_out))
                    dve.wait_ge(sm_exp, w(sm_exp, H2))
                    link(dve.reciprocal(hrec[:], hsum[:]))
                    for t in range(TT):
                        ins = dve.tensor_tensor(o[:, 1 + grp, t].rearrange("p (h n) -> p h n", h=H2),
                                                A[2 + t][:].rearrange("p (h n) -> p h n", h=H2),
                                                hrec[:, t].unsqueeze(2).to_broadcast([P, H2, DH]), ALU.mult)
                    ins.then_inc(heads_read, 1)
                merge()
                for c in range(D // CH):
                    for t in range(TT):
                        dve.wait_ge(out_projected, w(out_projected))
                        cols = slice(c * CH, (c + 1) * CH)
                        ins = dve.tensor_tensor(x[:, t, cols], x[:, t, cols], G[2 * c + t][:], ALU.add)
                ins.then_inc(x_updated, 1)
                norm_and_split(x, lambda k: gT[:, 1, bass.ds(l, 1), k], None)

                def up_down():
                    for t in range(TT):
                        dve.wait_ge(ff_relu, w(ff_relu))
                        dve.scalar_tensor_tensor(fsq[:, t], G[t][:], 0.0, frelu[:, t], ALU.max, ALU.mult).then_inc(ff_sq, 1)
                    split_low(two_kt(uhi, 4), two_kt(ulo, 4))

                with w.loop(FF // CH, {ff_relu.name: TT, split_hi.name: 2}) as i:
                    up_down()
                dve.wait_ge(ff_done, w(ff_done))
                for c, bank in enumerate((G[2], A[2], G[3], A[3])):
                    n, t = divmod(c, TT)
                    cols = slice(n * CH, (n + 1) * CH)
                    ins = dve.tensor_tensor(x[:, t, cols], x[:, t, cols], bank[:], ALU.add)
                ins.then_inc(x_updated, 1)

            with w.loop(DEPTH, LAYER_DVE) as l:
                layer(l)
            dve.wait_ge(rms_ready, w(rms_ready))
            link(dve.reciprocal(rstd[:, 0:TT], rms[:, 0:TT]))
            dve.wait_ge(final_in, w(final_in, 16))
            for t in range(TT):
                ins = dve.scalar_tensor_tensor(x[:, t], x[:, t], rstd[:, t:t + 1], gfin[:], ALU.mult, ALU.mult)
            ins.then_inc(out_ready, 1)

        @block.tensor
        def _(pe):
            w = Tally(pe)

            def product(bank, hi, lo, slot, kk, n, first, last):
                pe.matmul(bank, hi, whi[:, slot, kk, 0:n], start=first, stop=False)
                pe.matmul(bank, hi, wlo[:, slot, kk, 0:n], start=False, stop=False)
                return pe.matmul(bank, lo, whi[:, slot, kk, 0:n], start=False, stop=last)

            def chunk(banks, hi, lo, n=CH, free=None, tiles=TT, ready=projected):
                for s in range(SLOTS):
                    pe.wait_ge(lo_ready, w(lo_ready))
                    for t in range(tiles):
                        if s == 0 and free is not None:
                            pe.wait_ge(free, w(free))
                        for kk in range(SLAB_K):
                            k = s * SLAB_K + kk
                            cols = slice(t * P, (t + 1) * P)
                            ins = product(banks[t][:, 0:n], hi[:, k, cols], lo[:, k, cols], s, kk, n, k == 0, k == KT - 1)
                        if s == SLOTS - 1:
                            ins.then_inc(ready, 1)
                    if s < SLOTS - 1:
                        ins.then_inc(weights_used, 1)

            def turn_heads(blocks):
                count = (len(blocks) + 1) // 2
                for n in range(count):
                    if n >= 4:
                        pe.wait_ge(turned_copied, w(turned_copied))
                    for b, blk in enumerate(blocks[2 * n:2 * n + 2]):
                        for t in range(TT):
                            ins = pe.transpose(A[n % 4][:, b * S + t * P:b * S + (t + 1) * P], blk(t), ident[:])
                    ins.then_inc(turned, 1)
                pe.wait_ge(turned_copied, w(turned_copied, min(count, 4)))

            def turn_split(srcs):
                count = len(srcs) // 2
                for n in range(count):
                    if n >= 4:
                        pe.wait_ge(split_lo, w(split_lo))
                    for b in range(2):
                        for t in range(TT):
                            ins = pe.transpose(A[n % 4][:, b * S + t * P:b * S + (t + 1) * P], srcs[2 * n + b](t), ident[:])
                    ins.then_inc(split_turned, 1)
                pe.wait_ge(split_lo, w(split_lo, min(count, 4)))

            def turn_normed():
                pe.wait_ge(norm_ready, w(norm_ready, TT))
                for q in range(4):
                    for b in range(2):
                        k = 2 * q + b
                        for t in range(TT):
                            ins = pe.transpose(A[q][:, b * S + t * P:b * S + (t + 1) * P], normed[:, t, k * P:(k + 1) * P], ident[:])
                    ins.then_inc(h_turned, 1)
                pe.wait_ge(h_split, w(h_split, 4))

            def pair_counts(n):
                return {lo_ready.name: SLOTS * n, evacuated.name: TT * n}

            def merge(ready):
                pe.wait_ge(evacuated, w(evacuated, 2 * TT))
                turn_split([lambda t, b=b, k=k: o[:, b, t, k * P:(k + 1) * P] for b in range(3) for k in range(4)])
                for u in range(6):
                    b = u % 3
                    for s in range(2):
                        slot = 2 * (u % 2) + s
                        pe.wait_ge(lo_ready, w(lo_ready))
                        for t in range(TT):
                            if s == 0 and u >= 2:
                                pe.wait_ge(merged, w(merged))
                            for kk in range(SLAB_K):
                                k = s * SLAB_K + kk
                                cols = slice(t * P, (t + 1) * P)
                                ins = product(G[2 * (u % 2) + t][:], ohi[:, b, k, cols], olo[:, b, k, cols], slot, kk, CH,
                                              k == 0, k == 3)
                            if s == 1:
                                ins.then_inc(branch_out, 1)
                        if s == 0:
                            ins.then_inc(weights_used, 1)
                pe.wait_ge(merged, w(merged, 2 * TT))
                turn_split([lambda t, k=k: y[:, t, k * P:(k + 1) * P] for k in range(KT)])
                for n in range(D // CH):
                    chunk(G[2 * n:2 * n + 2], hhi, hlo, ready=ready)

            pe.wait_ge(consts_in, w(consts_in, 16 * N_CONST))
            pe.wait_ge(lo_ready, w(lo_ready, SLOTS))
            for is_x, l, full in PASSES:
                if not is_x:
                    pe.wait_ge(cond_split, w(cond_split))
                    pe.sem_inc(evacuated, 2)
                    with w.loop(3, {lo_ready.name: 2 * SLOTS, evacuated.name: 2}) as i:
                        for p in range(2):
                            chunk(G[p:p + 1], hhi, hlo, free=evacuated, tiles=1)
                    pe.wait_ge(evacuated, w(evacuated, 2))
                    pe.wait_ge(layer_in, w(layer_in, 16 * N_LAYER))
                    for b in range(4):
                        ins = pe.transpose(A[0][:, b * P:(b + 1) * P], wsin[:, b], ident[:])
                    ins.then_inc(ws_turned, 1)
                    pe.wait_ge(wsT_ready, w(wsT_ready))
                    pe.wait_ge(mod_ready, w(mod_ready))
                    for q in range(4):
                        for b in range(4):
                            at = (4 * q + b) * P
                            ins = pe.transpose(A[q][:, b * P:(b + 1) * P], mod[:, at:at + P], ident[:])
                        ins.then_inc(mod_turned, 1)
                    pe.wait_ge(modT_ready, w(modT_ready, 4))
                turn_normed()
                pe.sem_inc(evacuated, 2 * TT)
                with w.loop(2, pair_counts(2)) as i:
                    for p in range(2):
                        chunk(G[2 * p:2 * p + 2], hhi, hlo, free=evacuated)
                if full:
                    with w.loop(3, pair_counts(2)) as i:
                        for p in range(2):
                            chunk(G[2 * p:2 * p + 2], hhi, hlo, free=evacuated)
                    chunk(G[0:2], hhi, hlo, free=evacuated)
                pe.wait_ge(evacuated, w(evacuated, 2 * TT))
                if is_x:
                    pe.wait_ge(roped, w(roped))
                cols = (RK, RQ, DKc, DQ) if full else (DKc,)
                turn_heads([lambda t, c=c, h=h: z[:, t, c + h * P:c + (h + 1) * P] for c in cols for h in range(H1)])
                rkT, rqT, dkT, dqT = (tT[:, a] for a in range(4))
                if not is_x:
                    for h in range(H1):
                        pe.wait_ge(state_v, w(state_v))
                        for t in range(TT):
                            ins = pe.matmul(A[h][:, 0:2 * DK1], z[:, t, RK + h * DK1:RK + (h + 1) * DK1],
                                            e[:, h % 2, t, 0:2 * DK1], start=t == 0, stop=t == TT - 1)
                        ins.then_inc(state_sum, 1)
                    pe.wait_ge(state_copied, w(state_copied, H1))
                    pe.wait_ge(turned_copied, w(turned_copied, TT))
                if not full:
                    continue
                for i in range(H1 + 1):
                    if i < H1:
                        if i >= 2:
                            pe.wait_ge(ret_read, w(ret_read))
                        for j in range(TT):
                            ins = pe.matmul(A[i % 2][:, j * S:(j + 1) * S], rkT[:, i, j * P:(j + 1) * P], rqT[:, i],
                                            start=True, stop=True)
                        ins.then_inc(ret_scores, 1)
                        if is_x:
                            for t in range(TT):
                                ins = pe.matmul(A[2 + i % 2][:, t * S:(t + 1) * S], rqT[:, i, t * P:(t + 1) * P],
                                                state[:, i].rearrange("p d n -> p (d n)"), start=True, stop=True)
                            ins.then_inc(ret_cross, 1)
                    if i >= 1:
                        h = i - 1
                        pe.wait_ge(ret_weights, w(ret_weights))
                        for t in range(TT):
                            for j in range(TT):
                                ins = pe.matmul(A[h % 2][:, t * P:(t + 1) * P], e[:, h % 2, 0, j * S + t * P:j * S + (t + 1) * P],
                                                z[:, j, RV + h * DK1:RV + (h + 1) * DK1], start=j == 0, stop=j == TT - 1)
                        ins.then_inc(ret_out, 1)
                pe.wait_ge(ret_read, w(ret_read, 2))
                m = H1 * TT
                for i in range(m + 1):
                    if i < m:
                        h, t = divmod(i, TT)
                        if i >= 2:
                            pe.wait_ge(diff_read, w(diff_read))
                        for b in range(2):
                            half_p = slice(b * DH, (b + 1) * DH)
                            bank = A[2 * (i % 2) + b]
                            keys = [cdkT, dkT] if is_x else [dkT]
                            for c, kT in enumerate(keys):
                                ins = pe.matmul(bank[:, c * S:(c + 1) * S], dqT[half_p, h, t * P:(t + 1) * P], kT[half_p, h],
                                                start=True, stop=True)
                        ins.then_inc(diff_scores, 1)
                    if i >= 1:
                        j = i - 1
                        h = j // TT
                        nb = 4 if is_x else 2
                        pe.wait_ge(diff_mixed, w(diff_mixed))
                        for b in range(nb):
                            ins = pe.transpose(A[2 * (j % 2)][:, b * P:(b + 1) * P], e[:, j % 2, 0, b * P:(b + 1) * P], ident[:])
                        ins.then_inc(diff_turned, 1)
                        pe.wait_ge(diff_aT, w(diff_aT))
                        for b in range(nb):
                            val = cdv[:, b] if is_x and b < TT else z[:, b % TT, DV:DV + W]
                            ins = pe.matmul(A[2 * (j % 2) + 1][:, 0:P], aT[:, j % 2, b * P:(b + 1) * P], val[:, h * P:(h + 1) * P],
                                            start=b == 0, stop=b == nb - 1)
                        ins.then_inc(diff_out, 1)
                pe.wait_ge(diff_read, w(diff_read, 2))
                pe.wait_ge(mlp_vn, w(mlp_vn, TT))
                for t in range(TT):
                    for b in range(4):
                        ins = pe.matmul(A[t][:, b * P:(b + 1) * P], wsT[:, b], z[:, t, MV + b * P:MV + (b + 1) * P],
                                        start=True, stop=True)
                    ins.then_inc(mlp_mixed, 1)
                pe.wait_ge(branches_ready, w(branches_ready, 3))
                pe.sem_inc(evacuated, 2 * TT)
                with w.loop(3, pair_counts(2)) as i:
                    for p in range(2):
                        chunk(G[2 * p:2 * p + 2], hhi, hlo, free=evacuated)
                merge(projected)
                for c in range(D // CH):
                    pe.matmul(A[c][:], pick[:, 0 if is_x else 1], mgate[:, c * CH:(c + 1) * CH], start=True, stop=True)\
                      .then_inc(gate_spread, 1)
                pe.wait_ge(out_evacuated, w(out_evacuated, 2 * TT))
                pe.wait_ge(x_updated, w(x_updated))

            pe.wait_ge(gains_in, w(gains_in, 16))

            def layer(l):
                turn_normed()
                pe.sem_inc(evacuated, 2 * TT)
                with w.loop(3, pair_counts(2)) as i:
                    for p in range(2):
                        chunk(G[2 * p:2 * p + 2], hhi, hlo, free=evacuated)
                for n, (col, width) in enumerate(MID):
                    chunk(G[2 * (n % 2):2 * (n % 2) + 2], hhi, hlo, width, free=evacuated)
                pe.wait_ge(evacuated, w(evacuated, 2 * TT))
                pe.wait_ge(roped, w(roped))

                def head_block(c, n):
                    return lambda t: z2[:, t, c + n * P:c + (n + 1) * P]

                blocks = [head_block(c, n) for c in (QA, KA, QB, KB, QC) for n in range(4)]
                blocks += [head_block(QI, n) for n in range(2)] + [lambda t, n=n: dup[:, t, n] for n in range(3)]
                turn_heads(blocks)
                qa, ka, qb, kb, qc, qi = (t2[:, 4 * a:4 * a + 4] for a in range(6))
                kc, ki = t2[:, 22:24], t2[:, 24]

                def rows(h):
                    return slice((h % 2) * DH, (h % 2 + 1) * DH)

                def scores(bank, q, k, h):
                    pe.matmul(bank[:, 0:P], q[rows(h), 0:P], k[rows(h), 0:P], start=True, stop=False, skip_group_check=True)
                    return pe.matmul(bank[:, P:3 * P], q[rows(h), P:S], k[rows(h), 0:S], start=False, stop=False,
                                     skip_group_check=True)

                for h in range(NI):
                    pe.matmul(A[h][:, 0:P], qi[rows(h), h // 2, 0:P], ki[rows(h), 0:P], start=True, stop=True)
                    pe.matmul(A[h][:, P:3 * P], qi[rows(h), h // 2, P:S], ki[rows(h), 0:S], start=True, stop=True)\
                      .then_inc(idx_dots, 1)
                pe.wait_ge(idx_relu, w(idx_relu, NI))
                pe.wait_ge(forget_ready, w(forget_ready))
                pe.matmul(A[0][0:NF, 0:S], fg[:, 2, 0], upto[:, 0:S], start=True, stop=False, skip_group_check=True)
                pe.matmul(A[0][0:NF, P:S], fg[:, 2, 1], upto[:, 0:P], start=False, stop=True, skip_group_check=True).then_inc(cum_out, 1)
                pe.wait_ge(cum_copied, w(cum_copied))
                for i in range(H2 + 2):
                    if i >= 2:
                        j = i - 2
                        pe.wait_ge(sb_weights, w(sb_weights))
                        v = [z2[:, s, VA + j * DH:VA + (j + 1) * DH] for s in range(TT)]
                        cols = slice(j * DH, (j + 1) * DH)
                        pe.matmul(A[2][:, cols], tmp[:, j % 2, 3, 0:P], v[0], start=True, stop=True)
                        pe.matmul(A[3][:, cols], tmp[:, j % 2, 3, P:2 * P], v[0], start=True, stop=False)
                        ins = pe.matmul(A[3][:, cols], tmp[:, j % 2, 3, 2 * P:], v[1], start=False, stop=True)
                        if j == H2 - 1:
                            ins.then_inc(heads_out, 1)
                    if i < H2:
                        bank, q, k = A[i % 2], qa[:, i // 2], ka[:, i // 2]
                        pe.matmul(bank[:, 0:S], k[rows(i), 0:P], q[rows(i), 0:S], start=True, stop=False, skip_group_check=True)
                        pe.matmul(bank[:, S:3 * P], k[rows(i), P:S], q[rows(i), P:S], start=False, stop=False, skip_group_check=True)
                        pe.matmul(bank[:, 0:P], ident16, strict16, start=False, stop=False, skip_group_check=True)
                        pe.matmul(bank[:, S:3 * P], ident16, strict16, start=False, stop=True, skip_group_check=True)\
                          .then_inc(sb_scores, 1)
                    if 1 <= i <= H2:
                        j = i - 1
                        pe.wait_ge(sb_soft, w(sb_soft))
                        pe.matmul(A[j % 2][:, 0:3 * P], later[:], tmp[:, j % 2, 2], start=False, stop=False, skip_group_check=True)
                        pe.matmul(A[j % 2][:, P:S], every[:], tmp[:, j % 2, 2, S:3 * P], start=False, stop=True,
                                  skip_group_check=True).then_inc(sb_cum, 1)
                pe.wait_ge(heads_read, w(heads_read))
                for grp in range(2):
                    for i in range(H2 + 2):
                        if i >= 2:
                            j = i - 2
                            pe.wait_ge(sm_copied, w(sm_copied))
                            col = VB + j * DH if grp == 0 else VC + (j // 4) * DH
                            v = [z2[:, s, col:col + DH] for s in range(TT)]
                            cols = slice(j * DH, (j + 1) * DH)
                            pe.matmul(A[2][:, cols], tmp[:, j % 2, 1, 0:P], v[0], start=True, stop=True)
                            pe.matmul(A[3][:, cols], tmp[:, j % 2, 1, P:2 * P], v[0], start=True, stop=False)
                            ins = pe.matmul(A[3][:, cols], tmp[:, j % 2, 1, 2 * P:], v[1], start=False, stop=True)
                            if j == H2 - 1:
                                ins.then_inc(heads_out, 1)
                        if i < H2:
                            bank = A[i % 2]
                            if grp == 0:
                                scores(bank, qb[:, i // 2], kb[:, i // 2], i)
                                pe.matmul(bank[:, 0:P], esel[0:NF, i], negc[0:NF, 0:P], start=False, stop=False, skip_group_check=True)
                                pe.matmul(bank[:, P:3 * P], esel[0:NF, i], negc[0:NF, 0:S], start=False, stop=False, skip_group_check=True)
                            else:
                                if i == 0:
                                    pe.wait_ge(selected, w(selected))
                                scores(bank, qc[:, i // 2], kc[:, i // 4], i)
                                pe.matmul(bank[:, 0:3 * P], ident16, selb[:], start=False, stop=False, skip_group_check=True)
                            pe.matmul(bank[:, 0:P], ident16, causal16, start=False, stop=False, skip_group_check=True)
                            pe.matmul(bank[:, 2 * P:3 * P], ident16, causal16, start=False, stop=True, skip_group_check=True)\
                              .then_inc(sm_scores, 1)
                        if 1 <= i <= H2:
                            j = i - 1
                            pe.wait_ge(sm_exp, w(sm_exp))
                            for b in range(3):
                                ins = pe.transpose(A[j % 2][:, b * P:(b + 1) * P], tmp[:, j % 2, 0, b * P:(b + 1) * P], ident[:])
                            ins.then_inc(sm_turned, 1)
                    pe.wait_ge(heads_read, w(heads_read))
                pe.sem_inc(evacuated, 2 * TT)
                with w.loop(3, pair_counts(2)) as i:
                    for p in range(2):
                        chunk(G[2 * p:2 * p + 2], hhi, hlo, free=evacuated)
                merge(out_projected)
                pe.wait_ge(x_updated, w(x_updated))
                turn_normed()
                down = [[G[2], A[2]], [G[3], A[3]]]

                def up_down(first, last):
                    chunk(G[0:2], hhi, hlo)
                    pe.wait_ge(ff_sq, w(ff_sq, TT))
                    turn_split([lambda t, k=k: fsq[:, t, k * P:(k + 1) * P] for k in range(4)])
                    for n in range(D // CH):
                        for s in range(2):
                            pe.wait_ge(lo_ready, w(lo_ready))
                            for t in range(TT):
                                for kk in range(SLAB_K):
                                    k = s * SLAB_K + kk
                                    cols = slice(t * P, (t + 1) * P)
                                    ins = product(down[n][t][:], uhi[:, k, cols], ulo[:, k, cols], 2 * n + s, kk, CH,
                                                  first and k == 0, last and k == 3)
                            end = last and n == D // CH - 1 and s == 1
                            ins.then_inc(ff_done if end else weights_used, 1)

                up_down(True, False)
                per = {lo_ready.name: 2 * SLOTS, ff_sq.name: TT, split_lo.name: 2}
                with w.loop(FF // CH - 2, per) as i:
                    up_down(False, False)
                up_down(False, True)
                pe.wait_ge(x_updated, w(x_updated))

            with w.loop(DEPTH, LAYER_PE) as l:
                layer(l)


LAYER_ACT = {'raw_full0': 576, 'raw_full1': 576, 'raw_full2': 576, 'raw_full3': 576, 'weights_used': 112, 'projected': 46, 'act_step': 20, 'turned': 13, 'split_turned': 26, 'branch_out': 12, 'x_updated': 2, 'idx_dots': 4, 'forget_in': 1, 'forget_exp': 1, 'cum_out': 1, 'selected': 1, 'sb_scores': 8, 'sb_cum': 8, 'sm_max': 16, 'sm_turned': 16, 'heads_read': 3, 'out_projected': 4}
LAYER_DVE = {'dve_step': 76, 'evacuated': 38, 'rms_ready': 2, 'h_turned': 8, 'split_hi': 26, 'branch_out': 12, 'forget_log': 1, 'idx_relu': 4, 'sb_log': 8, 'heads_out': 3, 'sm_scores': 16, 'sm_exp': 16, 'out_projected': 4, 'ff_relu': 16, 'ff_done': 1}
LAYER_PE = {'lo_ready': 144, 'evacuated': 38, 'norm_ready': 4, 'h_split': 8, 'turned_copied': 13, 'split_lo': 26, 'merged': 12, 'x_updated': 2, 'roped': 1, 'idx_relu': 4, 'forget_ready': 1, 'cum_copied': 1, 'sb_soft': 8, 'sb_weights': 8, 'heads_read': 3, 'sm_exp': 16, 'sm_copied': 16, 'selected': 1, 'ff_sq': 16}

_INS = ["x", "c", "ctx", "c_ctx", "w_mod", "b_mod", "g_pre", "g_post", "w_in", "ret_decay_logit", "mlp_w_s", "mlp_b_s",
        "diff_lambda_q", "diff_lambda_k", "w_branch_out", "w_out", "positions_2", "g_mix_2", "w_in_2", "b_forget_2",
        "w_branch_2", "w_out_2", "g_mlp_2", "w_up_2", "w_down_2", "g_final_2"]


def kernel(**inputs):
    import concourse.bacc as bacc
    from concourse.bass_utils import run_bass_kernel_spmd

    nc = bacc.Bacc("TRN2", target_bir_lowering=False, num_devices=1)
    parts, dist, head, half = constants()
    arrays = {n: np.ascontiguousarray(inputs[n]) for n in _INS}
    arrays |= {"k_" + n: a for n, a in parts.items()} | {"k_dist": dist, "k_head": head, "k_half": half}
    arrays = {"in_" + n: np.ascontiguousarray(a) for n, a in arrays.items()}
    g = {n[3:]: nc.dram_tensor(n, a.shape, mybir.dt.from_np(a.dtype), kind="ExternalInput").ap() for n, a in arrays.items()}
    out = nc.dram_tensor("result", (1, S, D), F32, kind="ExternalOutput").ap()
    build(nc, g, out)
    return run_bass_kernel_spmd(nc, [arrays], core_ids=[0]).results[0]["result"]
```

```python
import math
from contextlib import ExitStack, contextmanager

import numpy as np

import concourse.bass as bass
from concourse import mybir

F32, F32R, BF16, I32 = mybir.dt.float32, mybir.dt.float32r, mybir.dt.bfloat16, mybir.dt.int32
ACT, ALU, AX = mybir.ActivationFunctionType, mybir.AluOpType, mybir.AxisListType

P = 128
D = 1024
S = 256
TT = S // P
KT = D // P
CH = 512
SLAB_K = 2
SLOTS = 4
DEPTH = 2
W = 512
EPS = 1e-6
NEG = -1e30
TAKEN = -3e38
H1, DK1 = 4, 128
H2, DH = 8, 64
TOPK = min(256, S // 4)
FF = 4 * D
ROT = DH // 8
NF, NI = 8, 4
IN1 = 11 * W + 3 * D
QA, KA, VA, QB, KB, VB, FL, QC, KC, VC, QI, KI, WI, GL = np.cumsum(
    [0, W, W, W, W, W, W, NF, W, 128, 128, 256, 64, NI]).tolist()
IN2 = GL + 3 * D
RK, RV, DKc, DV, RQ, RG, DQ, DG, MU, MV, MG = (i * W for i in range(11))


class Tally:

    def __init__(self, eng):
        self.eng, self.reg, self.num = eng, {}, {}

    def __call__(self, sem, n=1):
        name = sem.name
        self.num[name] = self.num.get(name, 0) + n
        reg = self.reg.get(name)
        return self.num[name] if reg is None else reg + self.num[name]

    @contextmanager
    def loop(self, trips, per):
        reg, num = dict(self.reg), dict(self.num)
        with self.eng.Fori(0, trips) as i:
            for name, n in per.items():
                self.reg[name] = i * n if name not in reg else reg[name] + i * n
            yield i
            now = {k: v - num.get(k, 0) for k, v in self.num.items() if v != num.get(k, 0)}
            assert now == per, f"a trip of {self.eng.engine} waits for {now}"
        self.reg = reg
        self.num = {**num, **{k: num.get(k, 0) + trips * n for k, n in per.items()}}


def constants():
    p = np.arange(P)
    tok = np.arange(S, dtype=np.float32)
    rows, cols = (np.arange(S) // 64).astype(np.float32), (np.arange(S) % 64).astype(np.float32)

    def angles(dim):
        n = dim // 4
        inv = (np.float32(10000.0) ** (-np.arange(n, dtype=np.float32) / np.float32(n))).astype(np.float32)
        ang = np.concatenate([rows[:, None] * inv, cols[:, None] * inv], axis=-1)
        both = np.stack([np.cos(ang), np.sin(ang)], axis=1).astype(np.float32)
        return both.reshape(TT, P, 2, dim // 2).transpose(1, 0, 2, 3).reshape(P, -1)

    reach = np.stack([np.stack([S - 1 - tok, tok]), np.stack([tok + 1, S - tok])])
    reach = reach.reshape(2, 2, TT, P).transpose(3, 2, 0, 1).reshape(P, -1)
    later = (p[:, None] >= p[None, :]).astype(np.float32)
    upto = (np.arange(P)[:, None] <= np.arange(S)[None, :]).astype(np.float32)
    inv2 = (np.float32(500000.0) ** (-np.arange(0, 2 * ROT, 2, dtype=np.float32) / np.float32(2 * ROT)))
    pick = np.zeros((P, 2, P), np.float32)
    pick[0, 0], pick[64, 1] = 1, 1
    parts = dict(
        ident=np.eye(P, dtype=np.float32), rope_r=angles(DK1), rope_d=angles(DH), reach=reach,
        later=-later, every=-np.ones((P, P), np.float32), upto=-upto,
        inv2=np.tile(inv2.astype(np.float32), (P, 1)), pick=pick.reshape(P, -1))
    j = np.arange(S).reshape(TT, P).T[:, :, None]
    i = np.arange(S)[None, None, :]
    f, b = i >= j, j >= i
    dist = np.stack([np.where(f, i - j, 0), np.where(b, j - i, 0),
                     f * DK1 ** -0.5, b * DK1 ** -0.5], axis=1).astype(np.float32)
    head = np.zeros((P, NF, P), np.float32)
    for h in range(NF):
        head[h, h] = 1
    half = np.stack([np.eye(P), np.where(p[None, :] > p[:, None], NEG, 0),
                     np.where(p[:, None] >= p[None, :], NEG, 0)], axis=1).astype(np.float32)
    return parts, dist.reshape(P, -1), head.reshape(P, -1), half.reshape(P, -1)


def build(nc, g, out):
    sizes = {k: v.shape[1] for k, v in constants()[0].items()}
    place = {"at": (nc.sbuf_base + 31) // 32 * 32}

    def sb_at(name, shape, dt, offset):
        return nc.alloc_sbuf_tensor_at(name, shape, dt, offset=offset)

    def sb(name, shape, dt=F32):
        size = int(np.prod(shape[1:])) * mybir.dt.size(dt)
        at = place["at"]
        place["at"] = at + (size + 31) // 32 * 32
        place[name] = at
        return sb_at(name, shape, dt, at)

    with ExitStack() as ctx:
        def sem(name):
            return ctx.enter_context(nc.semaphore(name))

        raw = sb("raw", [P, SLOTS, SLAB_K, CH])
        whi = sb("whi", [P, SLOTS, SLAB_K, CH], F32R)
        wlo = sb("wlo", [P, SLOTS, SLAB_K, CH], F32R)
        x = sb("x", [P, TT, D])
        cx = sb("cx", [P, TT, D])
        zb = place["at"]
        z = sb("z", [P, TT, 11 * W])
        z2 = sb_at("z2", [P, TT, GL], F32, zb)
        gates = sb_at("gates", [P, TT, 3 * D], F32, zb)
        y = sb_at("y", [P, TT, D], F32, zb + 24576)
        oproj = sb_at("oproj", [P, TT, D], F32, zb + 32768)
        mtmp = sb_at("mtmp", [P, TT, CH], F32, zb + 40960)
        mod = sb_at("mod", [P, 3 * D], F32, zb)
        modb = sb_at("modb", [P, 3 * D], F32, zb + 12288)
        gpre = sb_at("gpre", [P, D], F32, zb + 24576)
        gpost = sb_at("gpost", [P, D], F32, zb + 28672)
        dist = sb_at("dist", [P, 4, TT * S], F32, zb + 32768)
        wsin = sb_at("wsin", [P, 4, P], F32, zb + 40960)
        dq = sb_at("dq", [P, 4, DH], F32, zb + 43008)
        dk = sb_at("dk", [P, 4, DH], F32, zb + 44032)
        frelu = sb_at("frelu", [P, TT, CH], F32, zb)
        fsq = sb_at("fsq", [P, TT, CH], F32, zb + 4096)
        gfin = sb_at("gfin", [P, D], F32, zb + 24576)
        hhi = sb("hhi", [P, KT, S], F32R)
        hlo = sb("hlo", [P, KT, S], F32R)
        tb = place["at"]
        tT = sb("tT", [P, 4, H1, S])
        rtmp = sb("rtmp", [P, 4, W])
        decay = sb("decay", [P, H1, TT * S])
        hfull = sb_at("hfull", [P, KT, S], F32, tb)
        t2 = sb_at("t2", [P, 25, S], F32, tb)
        ohi = sb_at("ohi", [P, 3, 4, S], F32R, tb)
        olo = sb_at("olo", [P, 3, 4, S], F32R, tb + 12288)
        uhi = sb_at("uhi", [P, 4, S], F32R, tb + 8192)
        ulo = sb_at("ulo", [P, 4, S], F32R, tb + 12288)
        o = sb("o", [P, 3, TT, W])
        junk = sb_at("junk", [P, D], F32, place["o"])
        normed = sb_at("normed", [P, TT, D], F32, place["o"] + D * 4)
        cb = place["at"]
        state = sb("state", [P, H1, 2, DK1])
        cdkT = sb("cdkT", [P, H1, S])
        cdv = sb("cdv", [P, TT, W])
        esel = sb_at("esel", [P, NF, P], F32, cb)
        dup = sb_at("dup", [P, TT, 3, P], F32, cb + 4096)
        work = sb_at("work", [P, 3 * P], F32, cb + 7168)
        selb = sb_at("selb", [P, 3 * P], BF16, cb + 8704)
        rt2 = sb_at("rt2", [P, 4, 10 * ROT], F32, cb + 9472)
        negc = sb_at("negc", [P, S], F32, cb + 10752)
        eb = place["at"]
        e = sb("e", [P, 2, 2, CH])
        aT = sb("aT", [P, 2, CH])
        tmp = sb_at("tmp", [P, 2, 4, 3 * P], F32, eb)
        mgate = sb("mgate", [P, D])
        modT = sb("modT", [P, 2, KT, 2])
        wsT = sb("wsT", [P, 4, P])
        cst = {k: sb("c_" + k, [P, n]) for k, n in sizes.items()}
        half = sb("half", [P, 3, P], BF16)
        ident, later, every, upto = cst["ident"], cst["later"], cst["every"], cst["upto"]
        ident16, causal16, strict16 = half[:, 0], half[:, 1], half[:, 2]
        rope_r = cst["rope_r"][:].rearrange("p (t c n) -> p t c n", t=TT, c=2)
        rope_d = cst["rope_d"][:].rearrange("p (t c n) -> p t c n", t=TT, c=2)
        pick = cst["pick"][:].rearrange("p (a m) -> p a m", a=2)
        cT = sb("cT", [P, KT, 2])
        cThi = sb("cThi", [P, KT, 2], F32R)
        cTlo = sb("cTlo", [P, KT, 2])
        eps = sb("eps", [P, 1])
        one = sb("one", [P, 1])
        ss = sb("ss", [P, 16])
        rms = sb("rms", [P, 16])
        rstd = sb("rstd", [P, 16])
        lgt = sb("lgt", [P, 6, DEPTH * 8])
        lg = sb("lg", [P, DEPTH, 2, H1])
        reachv = sb("reachv", [P, 4, 2, H1])
        lam = sb("lam", [P, 4])
        nlam = sb("nlam", [P, DEPTH])
        bs = sb("bs", [P, DEPTH, 4])
        mx = sb("mx", [P, 2, 2])
        nmx = sb("nmx", [P, 2, 2])
        sums = sb("sums", [P, 2, 2])
        rsum = sb("rsum", [P, 2, 2])
        bst = sb("bst", [P, TT, 6])
        bag = sb("bag", [P, TT, 2])
        dev = sb("dev", [P, TT])
        gate2 = [sb_at(f"gate2_{n}", [P, TT, CH], F32, at) for n, at in enumerate((
            zb + 33792, zb + 37888, tb + 25600, place["cx"], place["cx"] + 4096, place["mgate"]))]
        assert TT * GL * 4 <= 33792
        bfg = sb("bfg", [P, DEPTH, NF])
        gT = sb("gT", [P, 2, DEPTH, KT])
        posi = sb("posi", [P, TT], I32)
        ang = sb("ang", [P, 4, TT, ROT])
        rope_2 = sb("rope_2", [P, TT, 2, ROT])
        fg = sb("fg", [P, 3, TT, NF])
        wis = sb("wis", [P, TT, NI])
        mx8 = sb("mx8", [P, TT, 8])
        hsum = sb("hsum", [P, TT, H2])
        hrec = sb("hrec", [P, TT, H2])
        assert place["at"] <= nc.sbuf_usable_end, (place["at"], nc.sbuf_usable_end)

        G = [ctx.enter_context(nc.psum_tensor(f"G{i}", [P, CH], F32)) for i in range(4)]
        A = [ctx.enter_context(nc.psum_tensor(f"A{i}", [P, CH], F32)) for i in range(4)]
        HB = [A[2], A[3], G[2], G[3]]
        UP = [[G[0], G[1]], [A[0], A[1]]]
        DOWN = [[G[2], A[2]], [G[3], A[3]]]

        consts_in, params_in, tokens_in = sem("consts_in"), sem("params_in"), sem("tokens_in")
        layer_in, tables_in, gains_in, final_in = sem("layer_in"), sem("tables_in"), sem("gains_in"), sem("final_in")
        raw_full = [sem(f"raw_full{i}") for i in range(SLOTS)]
        hi_ready, lo_ready, weights_used = sem("hi_ready"), sem("lo_ready"), sem("weights_used")
        eps_set = sem("eps_set")
        act_step, dve_step = sem("act_step"), sem("dve_step")
        silu_c, cond_split = sem("silu_c"), sem("cond_split")
        lg_exp, lg_ready, lam_dot, lam_exp = sem("lg_exp"), sem("lg_ready"), sem("lam_dot"), sem("lam_exp")
        ang_ready, sin_ready = sem("ang_ready"), sem("sin_ready")
        projected, evacuated, out_projected, out_evacuated = (sem(n) for n in (
            "projected", "evacuated", "out_projected", "out_evacuated"))
        mod_ready, mod_turned, modT_ready = sem("mod_ready"), sem("mod_turned"), sem("modT_ready")
        ws_turned, wsT_ready = sem("ws_turned"), sem("wsT_ready")
        decay_exp, decay_built, reach_arg, reach_ready = (sem(n) for n in (
            "decay_exp", "decay_built", "reach_arg", "reach_ready"))
        rms_ready, norm_ready, h_turned, h_high, h_split = (sem(n) for n in (
            "rms_ready", "norm_ready", "h_turned", "h_high", "h_split"))
        rstd_ready = sem("rstd_ready")
        ss_ready, x_updated = sem("ss_ready"), sem("x_updated")
        var_ready, dev_ready, topk_step = sem("var_ready"), sem("dev_ready"), sem("topk_step")
        roped, turned, turned_copied = sem("roped"), sem("turned"), sem("turned_copied")
        state_v, state_sum, state_copied = sem("state_v"), sem("state_sum"), sem("state_copied")
        ret_scores, ret_weights, ret_cross, ret_out, ret_read = (sem(n) for n in (
            "ret_scores", "ret_weights", "ret_cross", "ret_out", "ret_read"))
        diff_scores, diff_max, diff_exp, diff_mixed, diff_turned, diff_aT, diff_out, diff_read = (sem(n) for n in (
            "diff_scores", "diff_max", "diff_exp", "diff_mixed", "diff_turned", "diff_aT", "diff_out", "diff_read"))
        mlp_vn, mlp_mixed = sem("mlp_vn"), sem("mlp_mixed")
        branches_ready = sem("branches_ready")
        late_projected, late_evacuated, gates_ready = sem("late_projected"), sem("late_evacuated"), sem("gates_ready")
        split_turned, split_hi, split_lo = sem("split_turned"), sem("split_hi"), sem("split_lo")
        branch_out, merged, gate_spread = sem("branch_out"), sem("merged"), sem("gate_spread")
        idx_dots, idx_relu, selected = sem("idx_dots"), sem("idx_relu"), sem("selected")
        forget_in, forget_exp, forget_log, forget_ready, cum_out, cum_copied = (sem(n) for n in (
            "forget_in", "forget_exp", "forget_log", "forget_ready", "cum_out", "cum_copied"))
        sb_scores, sb_log, sb_soft, sb_cum, sb_weights = (sem(n) for n in (
            "sb_scores", "sb_log", "sb_soft", "sb_cum", "sb_weights"))
        sm_scores, sm_max, sm_exp, sm_turned, sm_copied = (sem(n) for n in (
            "sm_scores", "sm_max", "sm_exp", "sm_turned", "sm_copied"))
        heads_out, heads_read = sem("heads_out"), sem("heads_read")
        ff_relu, ff_sq, ff_done, out_ready, out_stored = (sem(n) for n in (
            "ff_relu", "ff_sq", "ff_done", "out_ready", "out_stored"))

        PASSES = [(False, 0, True), (True, 0, True), (False, 1, False), (True, 1, True)]
        N_CONST, N_PARAM, N_LAYER, N_TABLE = len(sizes) + 1, 11, 3, 2
        slabs = DEPTH * 6 * SLOTS + 3 * (17 * SLOTS + 12 + 8) + 4 * SLOTS + DEPTH * (15 * SLOTS + 12 + 8 + 8 * 8)
        assert slabs % SLOTS == 0
        MID = [(FL, CH), (FL + CH, CH), (FL + 2 * CH, GL - FL - 2 * CH)]

        LATE = [RG, DG, MU, MV, MG]
        LATE_DIFF = 4 * SLOTS - (H1 + 1) - H1 * TT
        LATE_SM = (7, 7)
        LATE_TOPK = 7 * SLOTS - H2 - sum(LATE_SM)

        block = ctx.enter_context(nc.Block())

        @block.sync
        def _(sp):
            w = Tally(sp)
            for k in sizes:
                sp.dma_start(cst[k][:], g["k_" + k]).then_inc(consts_in, 16)
            sp.dma_start(rtmp[:, 0, 0:3 * P], g["k_half"]).then_inc(consts_in, 16)
            with nc.allow_non_contiguous_dma("small parameters, once"):
                sp.dma_start(cT[:, :, 0], g["c"][0].rearrange("(k p) -> p k", p=P)).then_inc(params_in, 16)
                sp.dma_start(cT[:, :, 1], g["c_ctx"].rearrange("(k p) -> p k", p=P)).then_inc(params_in, 16)
                sp.dma_start(lgt[:, 0, :], g["ret_decay_logit"].rearrange("l d h -> (l d h)")
                             .partition_broadcast(P)).then_inc(params_in, 16)
                sp.dma_start(dq[:].rearrange("p a n -> p (a n)"), g["diff_lambda_q"].rearrange("l a n -> (l a n)")
                             .partition_broadcast(P)).then_inc(params_in, 16)
                sp.dma_start(dk[:].rearrange("p a n -> p (a n)"), g["diff_lambda_k"].rearrange("l a n -> (l a n)")
                             .partition_broadcast(P)).then_inc(params_in, 16)
                sp.dma_start(bs[:].rearrange("p l a -> p (l a)"), g["mlp_b_s"].rearrange("l a i -> i (l a)"))\
                    .then_inc(params_in, 16)
                sp.dma_start(bfg[:].rearrange("p l n -> p (l n)"), g["b_forget_2"].rearrange("l n -> (l n)")
                             .partition_broadcast(P)).then_inc(params_in, 16)
                sp.dma_start(gT[:, 0].rearrange("p l k -> p (l k)"),
                             g["g_mix_2"].rearrange("l (k p) -> p (l k)", p=P)).then_inc(params_in, 16)
                sp.dma_start(gT[:, 1].rearrange("p l k -> p (l k)"),
                             g["g_mlp_2"].rearrange("l (k p) -> p (l k)", p=P)).then_inc(params_in, 16)
                sp.dma_start(posi[:, 0:1], g["positions_2"][0, 0:P].rearrange("(p a) -> p a", a=1)).then_inc(params_in, 16)
                sp.dma_start(posi[:, 1:2], g["positions_2"][0, P:S].rearrange("(p a) -> p a", a=1)).then_inc(params_in, 16)
            sp.dma_start(cx[:], g["ctx"][0].rearrange("(t p) d -> p t d", p=P)).then_inc(tokens_in, 16)
            sp.dma_start(x[:], g["x"][0].rearrange("(t p) d -> p t d", p=P)).then_inc(tokens_in, 16)

            def slab(mat, row, col, slot, n=CH):
                sp.wait_ge(lo_ready, w(lo_ready))
                src = mat[bass.ds(row, SLAB_K * P), bass.ds(col, n)].rearrange("(k p) n -> p k n", p=P)
                sp.dma_start(raw[:, slot, :, 0:n], src).then_inc(raw_full[slot], 16)

            def chunk(mat, row, col, n=CH):
                for s in range(SLOTS):
                    slab(mat, row + s * SLAB_K * P, col, s, n)

            def merge(wb, wo, row_b, row_o):
                for u in range(6):
                    for s in range(2):
                        slab(wb, row_b + (u % 3) * W + s * SLAB_K * P, (u // 3) * CH, 2 * (u % 2) + s)
                for n in range(D // CH):
                    chunk(wo, row_o, n * CH)

            flat = {k: g[k].rearrange("l r n -> (l r) n") for k in (
                "w_mod", "w_in", "w_out", "w_in_2", "w_out_2", "w_up_2", "w_down_2")}
            flat |= {k: g[k].rearrange("l b r n -> (l b r) n") for k in ("w_branch_out", "w_branch_2")}
            for is_x, l, full in PASSES:
                if not is_x:
                    with w.loop(3 * D // CH, {lo_ready.name: SLOTS}) as i:
                        chunk(flat["w_mod"], l * D, i * CH)
                if full:
                    with w.loop(2, {lo_ready.name: 2 * SLOTS}) as i:
                        for c in (RK, RQ):
                            chunk(flat["w_in"], l * D, i * (2 * W) + c)
                    with w.loop(2, {lo_ready.name: 2 * SLOTS}) as i:
                        for c in (RV, DV):
                            chunk(flat["w_in"], l * D, i * (4 * W) + c)
                    with w.loop((IN1 - MU) // CH, {lo_ready.name: SLOTS}) as i:
                        chunk(flat["w_in"], l * D, i * CH + MU)
                else:
                    with w.loop(4, {lo_ready.name: SLOTS}) as i:
                        chunk(flat["w_in"], l * D, i * CH)
                if full:
                    merge(flat["w_branch_out"], flat["w_out"], l * 3 * W, l * D)
            with w.loop(DEPTH, {lo_ready.name: 15 * SLOTS + 12 + 8 + 8 * 8}) as l:
                with w.loop(5, {lo_ready.name: SLOTS}) as i:
                    chunk(flat["w_in_2"], l * D, i * CH)
                for col, n in MID:
                    chunk(flat["w_in_2"], l * D, col, n)
                chunk(flat["w_in_2"], l * D, VB)
                with w.loop(6, {lo_ready.name: SLOTS}) as i:
                    chunk(flat["w_in_2"], l * D, i * CH + GL)
                merge(flat["w_branch_2"], flat["w_out_2"], l * 3 * W, l * D)

                def down(row):
                    for n in range(D // CH):
                        for s in range(2):
                            slab(flat["w_down_2"], row + s * SLAB_K * P, n * CH, 2 * n + s)

                chunk(flat["w_up_2"], l * D, 0)
                with w.loop(FF // CH - 1, {lo_ready.name: 2 * SLOTS}) as i:
                    chunk(flat["w_up_2"], l * D, i * CH + CH)
                    down(l * FF + i * CH)
                down(l * FF + FF - CH)
            sp.wait_ge(out_ready, w(out_ready))
            sp.dma_start(out[0].rearrange("(t p) d -> p t d", p=P), x[:]).then_inc(out_stored, 16)
            sp.wait_ge(out_stored, w(out_stored, 16))

        @block.gpsimd
        def _(pool):
            w = Tally(pool)
            pool.memset(wlo[:].bitcast(F32), 0.0).then_inc(lo_ready, SLOTS)
            with w.loop(slabs // SLOTS, {hi_ready.name: SLOTS}) as i:
                for s in range(SLOTS):
                    pool.wait_ge(hi_ready, w(hi_ready))
                    pool.tensor_tensor(wlo[:, s], raw[:, s], whi[:, s].bitcast(F32), ALU.subtract).then_inc(lo_ready, 1)

        @block.scalar
        def _(act):
            w = Tally(act)

            def link(ins):
                ins.then_inc(act_step, 1)
                act.wait_ge(act_step, w(act_step))

            def split(slot):
                act.wait_ge(raw_full[slot], w(raw_full[slot], 16))
                act.activation(whi[:, slot], raw[:, slot], ACT.Copy).then_inc(hi_ready, 1)

            def split_chunk_but_last():
                for s in range(SLOTS - 1):
                    act.wait_ge(weights_used, w(weights_used))
                    split(s)

            def evacuate(p, dst, func, scale=None):
                split_chunk_but_last()
                for t in range(TT):
                    act.wait_ge(projected, w(projected))
                    act.activation(dst[t], G[2 * p + t][:, 0:dst[t].shape[-1]], func, scale=1.0 if scale is None else scale[t])\
                       .then_inc(evacuated, 1)
                split(SLOTS - 1)

            def late_slab(n, dst, func=ACT.Copy, scale=None):
                c, s = divmod(n, SLOTS)
                if s < SLOTS - 1:
                    act.wait_ge(weights_used, w(weights_used))
                else:
                    for t in range(TT):
                        act.wait_ge(late_projected, w(late_projected))
                        act.activation(dst[c][t], G[2 * (c % 2) + t][:], func, scale=1.0 if scale is None else scale[t])\
                           .then_inc(late_evacuated, 1)
                split(s)

            def pair_counts(n_chunks):
                d = {weights_used.name: 3 * n_chunks, projected.name: TT * n_chunks}
                return d | {raw_full[s].name: 16 * n_chunks for s in range(SLOTS)}

            def columns(dst, c):
                return [dst[:, t, bass.ds(c, CH)] for t in range(TT)]

            def norm(src):
                for t in range(TT):
                    ins = act.activation(junk[:], src[:, t], ACT.Square, accum_out=ss[:, t:t + 1])
                    link(ins)
                act.activation(rms[:, 0:TT], ss[:, 0:TT], ACT.Sqrt, bias=eps[:], scale=1.0 / D).then_inc(rms_ready, 1)

            def turned_high(scale, shift):
                for q in range(4):
                    act.wait_ge(h_turned, w(h_turned))
                    for k in range(2 * q, 2 * q + 2):
                        part = HB[q][:, (k % 2) * S:(k % 2 + 1) * S]
                        if shift is None:
                            ins = act.activation(hhi[:, k], part, ACT.Copy, scale=scale(k))
                        else:
                            ins = act.activation(hhi[:, k], part, ACT.Identity, scale=scale(k), bias=shift(k))
                    ins.then_inc(h_high, 1)

            def copy_turned(dsts, scales):
                for n, (dst, scale) in enumerate(zip(dsts, scales)):
                    act.wait_ge(turned, w(turned))
                    act.activation(dst, A[n % 4][:, 0:dst.shape[-1]], ACT.Copy, scale=scale).then_inc(turned_copied, 1)

            def split_high(dsts, bank=0):
                for n, dst in enumerate(dsts, bank):
                    act.wait_ge(split_turned, w(split_turned))
                    act.activation(dst, A[n % 4][:], ACT.Copy).then_inc(split_hi, 1)

            def two_kt(buf, n=KT):
                return [buf[:, 2 * q:2 * q + 2, :].rearrange("p k s -> p (k s)") for q in range(n // 2)]

            def merge(more, in_first):
                for u in range(6):
                    act.wait_ge(weights_used, w(weights_used))
                    split(2 * (u % 2))
                    act.wait_ge(branch_out, w(branch_out, TT))
                    split(2 * (u % 2) + 1)
                    if u == 4:
                        split_high(two_kt(hhi)[0:2])
                for n in range(D // CH):
                    for s in range(SLOTS - 1):
                        if n == 0 and s == 2:
                            split_high(two_kt(hhi)[2:4], 2)
                        act.wait_ge(weights_used, w(weights_used))
                        if more or n == 0:
                            split(s)
                    if in_first:
                        for t in range(TT):
                            act.wait_ge(projected, w(projected))
                            act.activation(oproj[:, t, n * CH:(n + 1) * CH], G[2 * n + t][:], ACT.Copy).then_inc(out_evacuated, 1)
                    else:
                        act.wait_ge(out_projected, w(out_projected, TT))
                    if more or n == 0:
                        split(SLOTS - 1)

            act.wait_ge(eps_set, w(eps_set, 2))
            act.wait_ge(params_in, w(params_in, 16 * N_PARAM))
            act.activation(cT[:].rearrange("p k a -> p (k a)"), cT[:].rearrange("p k a -> p (k a)"), ACT.Silu)\
               .then_inc(silu_c, 1)
            act.wait_ge(lg_ready, w(lg_ready))
            act.activation(lgt[:, 2], lgt[:, 1], ACT.Exp, scale=-1.0).then_inc(lg_exp, 1)
            act.wait_ge(lam_dot, w(lam_dot))
            act.activation(lam[:], lam[:], ACT.Exp).then_inc(lam_exp, 1)
            act.wait_ge(ang_ready, w(ang_ready))
            act.activation(rope_2[:, :, 0, :], ang[:, 3], ACT.Sin)
            act.activation(rope_2[:, :, 1, :], ang[:, 2], ACT.Sin).then_inc(sin_ready, 1)
            for s in range(SLOTS):
                split(s)
            act.wait_ge(tokens_in, w(tokens_in, 32))
            act.wait_ge(lg_ready, w(lg_ready))
            norm(cx)

            for n, (is_x, l, full) in enumerate(PASSES):
                if not is_x:
                    act.dma_start(modb[:], g["b_mod"][l].partition_broadcast(P)).then_inc(layer_in, 16)
                    act.dma_start(gpre[:], g["g_pre"][l].partition_broadcast(P)).then_inc(layer_in, 16)
                    act.dma_start(gpost[:], g["g_post"][l].partition_broadcast(P)).then_inc(layer_in, 16)
                    per = {weights_used.name: 6, projected.name: 2} | {raw_full[s].name: 32 for s in range(SLOTS)}
                    with w.loop(3, per) as i:
                        for p in range(2):
                            split_chunk_but_last()
                            act.wait_ge(projected, w(projected))
                            act.activation(mod[:, bass.ds(i * (2 * CH) + p * CH, CH)], G[p][:], ACT.Copy).then_inc(evacuated, 1)
                            split(SLOTS - 1)
                    if n > 0:
                        act.wait_ge(x_updated, w(x_updated))
                    act.dma_start(dist[:].rearrange("p a n -> p (a n)"), g["k_dist"]).then_inc(tables_in, 16)
                    act.dma_start(wsin[:], g["mlp_w_s"][l].rearrange("a i j -> i a j")).then_inc(tables_in, 16)
                    for q in range(4):
                        act.wait_ge(mod_turned, w(mod_turned))
                        act.activation(modT[:, q // 2, 4 * (q % 2):4 * (q % 2) + 4, :],
                                       G[q][:].rearrange("p (k m) -> p k m", k=4)[:, :, 0::64], ACT.Copy).then_inc(modT_ready, 1)
                    act.wait_ge(modT_ready, w(modT_ready, 4))
                a = 0 if is_x else 1
                turned_high(lambda k: modT[:, 1, k, a:a + 1], lambda k: modT[:, 0, k, a:a + 1])
                if not is_x:
                    act.wait_ge(tables_in, w(tables_in, 16 * N_TABLE))
                    for h in range(H1):
                        if h >= 2:
                            act.wait_ge(decay_built, w(decay_built))
                        act.activation(e[:, h % 2, 0], dist[:, 0], ACT.Exp, scale=lg[:, l, 0, h:h + 1])
                        act.activation(e[:, h % 2, 1], dist[:, 1], ACT.Exp, scale=lg[:, l, 1, h:h + 1]).then_inc(decay_exp, 1)
                    act.wait_ge(decay_built, w(decay_built, 2))
                    act.wait_ge(reach_arg, w(reach_arg))
                    act.activation(reachv[:].rearrange("p a d h -> p (a d h)"), reachv[:].rearrange("p a d h -> p (a d h)"),
                                   ACT.Exp).then_inc(reach_ready, 1)
                if n == 1:
                    norm(oproj)
                    act.wait_ge(x_updated, w(x_updated))
                if n == 2:
                    norm(x)
                with w.loop(2, pair_counts(2)) as i:
                    evacuate(0, columns(z, i * (2 * W) + RK), ACT.Copy)
                    evacuate(1, columns(z, i * (2 * W) + (RQ if full else RV)), ACT.Copy)
                if not is_x:
                    act.wait_ge(ws_turned, w(ws_turned))
                    act.activation(wsT[:].rearrange("p a i -> p (a i)"), A[0][:], ACT.Copy).then_inc(wsT_ready, 1)
                if full:
                    evacuate(0, columns(z, RV), ACT.Copy)
                    evacuate(1, columns(z, DV), ACT.Copy)
                late_dst = [columns(z, c) for c in LATE]
                if full:
                    copy_turned([tT[:, a, 2 * b:2 * b + 2].rearrange("p h s -> p (h s)") for a in range(4) for b in range(2)],
                                [1.0] * 8)
                else:
                    copy_turned([cdkT[:, 2 * b:2 * b + 2].rearrange("p h s -> p (h s)") for b in range(2)], [1.0] * 2)
                if not is_x:
                    if full:
                        act.wait_ge(turned_copied, w(turned_copied, 8))
                        act.activation(cdkT[:].rearrange("p h s -> p (h s)"), tT[:, 2].rearrange("p h s -> p (h s)"), ACT.Copy)
                    for t in range(TT):
                        act.activation(cdv[:, t], z[:, t, DV:DV + W], ACT.Copy).then_inc(turned_copied, 1)
                    for h in range(H1):
                        act.wait_ge(state_sum, w(state_sum))
                        act.activation(state[:, h].rearrange("p d n -> p (d n)"), A[h % 4][:, 0:2 * DK1], ACT.Copy,
                                       scale=DK1 ** -0.5).then_inc(state_copied, 1)
                if not full:
                    continue
                for i in range(H1 + 1):
                    late_slab(i, late_dst)
                m = H1 * TT
                nk = 2 * S if is_x else S
                late = H1 + 1
                for i in range(m + 2):
                    if i >= 2:
                        h, t = divmod(i - 2, TT)
                        act.wait_ge(diff_out, w(diff_out))
                        act.activation(o[:, 2, t, h * P:(h + 1) * P], A[2 * (i % 2) + 1][:, 0:P], ACT.Copy).then_inc(diff_read, 1)
                    if i < m:
                        act.wait_ge(diff_max, w(diff_max))
                        for b in range(2):
                            ins = act.activation(e[:, i % 2, b, 0:nk], A[2 * (i % 2) + b][:, 0:nk], ACT.Exp, scale=DH ** -0.5,
                                                 bias=nmx[:, i % 2, b:b + 1], accum_out=sums[:, i % 2, b:b + 1])
                        ins.then_inc(diff_exp, 1)
                        late_slab(late, late_dst)
                        late += 1
                    if 1 <= i <= m:
                        j = i - 1
                        act.wait_ge(diff_turned, w(diff_turned))
                        act.activation(aT[:, j % 2, 0:nk], A[2 * (j % 2)][:, 0:nk], ACT.Copy).then_inc(diff_aT, 1)
                        if j < LATE_DIFF:
                            late_slab(late, late_dst)
                            late += 1
                act.wait_ge(var_ready, w(var_ready))
                act.activation(dev[:], bag[:, :, 1], ACT.Sqrt, bias=eps[:]).then_inc(dev_ready, 1)
                act.wait_ge(ss_ready, w(ss_ready))
                act.activation(rms[:], ss[:], ACT.Sqrt, bias=eps[:], scale=1.0 / P).then_inc(rms_ready, 1)
                act.wait_ge(late_evacuated, w(late_evacuated, 4 * TT))
                for c in (RG, DG):
                    act.activation(z[:, :, c:c + W], z[:, :, c:c + W], ACT.Silu).then_inc(gates_ready, 1)
                while late < len(LATE) * SLOTS:
                    late_slab(late, late_dst, ACT.Silu)
                    late += 1
                act.wait_ge(late_evacuated, w(late_evacuated, TT))
                split_high([ap for b in range(3) for ap in two_kt(ohi[:, b], 4)])
                if n < 2:
                    norm(cx if is_x else x)
                act.wait_ge(branches_ready, w(branches_ready, 3))
                with w.loop(3, pair_counts(2)) as i:
                    for p in range(2):
                        evacuate(p, columns(gates, i * (2 * CH) + p * CH), ACT.Sigmoid)
                last = n == len(PASSES) - 1
                merge(not last, True)
                act.wait_ge(out_evacuated, w(out_evacuated, 2 * TT))
                if is_x:
                    norm(oproj)
            act.wait_ge(x_updated, w(x_updated))
            act.dma_start(esel[:].rearrange("p a n -> p (a n)"), g["k_head"]).then_inc(gains_in, 16)

            def layer(l):
                late_dst = [[z2[:, t, VB:VB + W] for t in range(TT)]] + [[gate2[n][:, t] for t in range(TT)] for n in range(6)]
                for s in range(SLOTS):
                    split(s)
                turned_high(lambda k: gT[:, 0, bass.ds(l, 1), k], None)
                norm(x)
                act.wait_ge(rstd_ready, w(rstd_ready))
                scale = [rstd[:, t:t + 1] for t in range(TT)]
                with w.loop(2, pair_counts(2)) as i:
                    for p in range(2):
                        evacuate(p, columns(z2, i * (2 * CH) + p * CH), ACT.Copy, scale)
                evacuate(0, [z2[:, t, KB:KB + W] for t in range(TT)], ACT.Copy, scale)
                for n, (col, width) in enumerate(MID, 1):
                    evacuate(n % 2, [z2[:, t, col:col + width] for t in range(TT)], ACT.Copy, scale)
                copy_turned([t2[:, 2 * n:min(2 * n + 2, 25)].rearrange("p b s -> p (b s)") for n in range(13)],
                            [DH ** -0.5] * 2 + [1.0] * 2 + [DH ** -0.5] * 2 + [1.0] * 2 + [DH ** -0.5] * 2 + [1.0] * 3)
                for h in range(NI):
                    act.wait_ge(idx_dots, w(idx_dots))
                    act.activation(tmp[:, h % 2, h // 2], A[h][:, 0:3 * P], ACT.Relu).then_inc(idx_relu, 1)
                act.wait_ge(forget_in, w(forget_in))
                act.activation(fg[:, 1], fg[:, 1], ACT.Exp, scale=-1.0).then_inc(forget_exp, 1)
                act.wait_ge(forget_exp, w(forget_exp))
                act.activation(fg[:, 1], fg[:, 1], ACT.Ln, bias=one[:]).then_inc(forget_log, 1)
                act.wait_ge(cum_out, w(cum_out))
                act.activation(negc[0:NF, :], A[0][0:NF, 0:S], ACT.Copy).then_inc(cum_copied, 1)
                for n in range(LATE_TOPK):
                    late_slab(n, late_dst, scale=scale)
                act.wait_ge(selected, w(selected))
                late = LATE_TOPK
                for i in range(H2 + 1):
                    if i < H2:
                        act.wait_ge(sb_scores, w(sb_scores))
                        link(act.activation(tmp[:, i % 2, 0], A[i % 2][:, 0:3 * P], ACT.Abs))
                        link(act.activation(tmp[:, i % 2, 0], tmp[:, i % 2, 0], ACT.Exp, scale=-1.0))
                        act.activation(tmp[:, i % 2, 1], tmp[:, i % 2, 0], ACT.Ln, bias=one[:]).then_inc(sb_log, 1)
                        late_slab(late, late_dst, scale=scale)
                        late += 1
                    if i >= 1:
                        j = i - 1
                        act.wait_ge(sb_cum, w(sb_cum))
                        act.activation(tmp[:, j % 2, 3], A[j % 2][:, 0:3 * P], ACT.Exp).then_inc(sb_weights, 1)
                for grp in range(2):
                    for i in range(H2 + 1):
                        if i < H2:
                            act.wait_ge(sm_max, w(sm_max))
                            act.activation(tmp[:, i % 2, 0, 0:P], A[i % 2][:, 0:P], ACT.Exp, bias=nmx[:, i % 2, 0:1],
                                           accum_out=hsum[:, 0, i:i + 1])
                            act.activation(tmp[:, i % 2, 0, P:3 * P], A[i % 2][:, P:3 * P], ACT.Exp, bias=nmx[:, i % 2, 1:2],
                                           accum_out=hsum[:, 1, i:i + 1]).then_inc(sm_exp, 1)
                            if i < LATE_SM[grp]:
                                late_slab(late, late_dst, scale=scale)
                                late += 1
                        if i >= 1:
                            j = i - 1
                            act.wait_ge(sm_turned, w(sm_turned))
                            act.activation(tmp[:, j % 2, 1], A[j % 2][:, 0:3 * P], ACT.Copy).then_inc(sm_copied, 1)
                    if grp == 0:
                        act.wait_ge(heads_read, w(heads_read, 2))
                act.wait_ge(heads_read, w(heads_read))
                split_high([ap for b in range(3) for ap in two_kt(ohi[:, b], 4)])
                act.wait_ge(late_evacuated, w(late_evacuated, 7 * TT))
                for n in range(2):
                    for b in range(3):
                        act.activation(gate2[2 * b + n][:], gate2[2 * b + n][:], ACT.Sigmoid).then_inc(gates_ready, 1)
                merge(True, False)
                turned_high(lambda k: gT[:, 1, bass.ds(l, 1), k], None)
                act.wait_ge(x_updated, w(x_updated, 2))
                norm(x)
                act.wait_ge(rstd_ready, w(rstd_ready))

                def relu(j):
                    for t in range(TT):
                        act.wait_ge(projected, w(projected))
                        act.activation(frelu[:, t], UP[j % 2][t][:], ACT.Relu, scale=scale[t]).then_inc(ff_relu, 1)

                def step(j):
                    for s in range(2):
                        act.wait_ge(weights_used, w(weights_used))
                        split(s)
                    squared_high(j)
                    act.wait_ge(weights_used, w(weights_used))
                    split(2)
                    relu(j + 1)
                    split(3)
                    for s in range(SLOTS):
                        act.wait_ge(weights_used, w(weights_used))
                        split(s)

                def squared_high(j):
                    for n, dst in enumerate(two_kt(uhi, 4)):
                        act.wait_ge(split_turned, w(split_turned))
                        act.activation(dst, UP[j % 2][n][:], ACT.Copy).then_inc(split_hi, 1)

                split_chunk_but_last()
                relu(0)
                split(SLOTS - 1)
                step(0)
                per = {weights_used.name: 14, projected.name: 2 * TT, split_turned.name: 4}
                per |= {raw_full[s].name: 64 for s in range(SLOTS)}
                with w.loop(FF // CH // 2 - 1, per) as i:
                    step(1)
                    step(2)
                squared_high(FF // CH - 1)
                for s in range(SLOTS - 1):
                    act.wait_ge(weights_used, w(weights_used))
                act.wait_ge(x_updated, w(x_updated, 2))

            with w.loop(DEPTH, LAYER_ACT) as l:
                layer(l)
            act.dma_start(gfin[:], g["g_final_2"].partition_broadcast(P)).then_inc(final_in, 16)
            norm(x)

        @block.vector
        def _(dve):
            w = Tally(dve)

            def link(ins):
                ins.then_inc(dve_step, 1)
                dve.wait_ge(dve_step, w(dve_step))

            def norm(src):
                dve.wait_ge(rms_ready, w(rms_ready))
                link(dve.reciprocal(rstd[:, 0:TT], rms[:, 0:TT]))
                for t in range(TT):
                    dve.tensor_scalar(normed[:, t], src[:, t], rstd[:, t:t + 1], None, ALU.mult).then_inc(norm_ready, 1)

            def turned_low(scale, shift):
                for q in range(4):
                    dve.wait_ge(h_high, w(h_high))
                    parts = [(k, HB[q][:, (k % 2) * S:(k % 2 + 1) * S]) for k in range(2 * q, 2 * q + 2)]
                    if shift is not None:
                        for k, part in parts:
                            ins = dve.tensor_scalar(hfull[:, k], part, scale(k), shift(k), ALU.mult, ALU.add)
                        link(ins)
                        both = slice(2 * q, 2 * q + 2)
                        ins = dve.tensor_tensor(hlo[:, both], hfull[:, both], hhi[:, both].bitcast(F32), ALU.subtract)
                    else:
                        for k, part in parts:
                            ins = dve.scalar_tensor_tensor(hlo[:, k], part, scale(k), hhi[:, k].bitcast(F32),
                                                           ALU.mult, ALU.subtract)
                    ins.then_inc(h_split, 1)

            def token_scale():
                dve.wait_ge(rms_ready, w(rms_ready))
                dve.reciprocal(rstd[:, 0:TT], rms[:, 0:TT]).then_inc(rstd_ready, 1)

            def spread_conditions():
                for a in range(2):
                    cols = slice(64 * a, 64 * a + 64)
                    dve.tensor_copy(hhi[:, :, cols], cThi[:, :, a:a + 1].bitcast(F32).to_broadcast([P, KT, 64]))
                    ins = dve.tensor_copy(hlo[:, :, cols], cTlo[:, :, a:a + 1].to_broadcast([P, KT, 64]))
                ins.then_inc(cond_split, 1)

            def residual(src):
                dve.wait_ge(rms_ready, w(rms_ready))
                link(dve.reciprocal(rstd[:, 0:TT], rms[:, 0:TT]))
                for c in range(D // CH):
                    dve.wait_ge(gate_spread, w(gate_spread))
                    for t in range(TT):
                        cols = slice(c * CH, (c + 1) * CH)
                        link(dve.scalar_tensor_tensor(mtmp[:, t], oproj[:, t, cols], rstd[:, t:t + 1], A[c][:],
                                                      ALU.mult, ALU.mult))
                        ins = dve.tensor_tensor(src[:, t, cols], src[:, t, cols], mtmp[:, t], ALU.add)
                    if c == 0:
                        link(ins)
                ins.then_inc(x_updated, 1)

            def split_low(dst_hi, dst_lo, bank=0):
                for n, (hi, lo) in enumerate(zip(dst_hi, dst_lo), bank):
                    dve.wait_ge(split_hi, w(split_hi))
                    dve.tensor_tensor(lo, A[n % 4][:], hi.bitcast(F32), ALU.subtract).then_inc(split_lo, 1)

            def two_kt(buf, n=KT):
                return [buf[:, 2 * q:2 * q + 2, :].rearrange("p k s -> p (k s)") for q in range(n // 2)]

            def rotate(x1, x2, cos, sin, temps):
                a, b, c, d = temps
                dve.tensor_tensor(a, x1, cos, ALU.mult)
                dve.tensor_tensor(b, x2, sin, ALU.mult)
                dve.tensor_tensor(c, x1, sin, ALU.mult)
                link(dve.tensor_tensor(d, x2, cos, ALU.mult))
                dve.tensor_tensor(x1, a, b, ALU.subtract)
                return dve.tensor_tensor(x2, c, d, ALU.add)

            def merge(in_first, then_norm=None):
                split_low([ap for b in range(3) for ap in two_kt(ohi[:, b], 4)],
                          [ap for b in range(3) for ap in two_kt(olo[:, b], 4)])
                if then_norm is not None:
                    norm(then_norm)
                if in_first:
                    dve.wait_ge(evacuated, w(evacuated, 2 * TT + 6 * TT))
                for u in range(6):
                    n, b = divmod(u, 3)
                    if not in_first:
                        dve.wait_ge(gates_ready, w(gates_ready))
                    for t in range(TT):
                        dve.wait_ge(branch_out, w(branch_out))
                        part = y[:, t, n * CH:(n + 1) * CH]
                        gate = gates[:, t, b * D + n * CH:b * D + (n + 1) * CH] if in_first else gate2[2 * b + n][:, t]
                        bank = G[2 * (u % 2) + t]
                        if b == 0:
                            dve.tensor_tensor(part, bank[:], gate, ALU.mult).then_inc(merged, 1)
                        else:
                            link(dve.tensor_tensor(e[:, u % 2, t], bank[:], gate, ALU.mult))
                            dve.tensor_tensor(part, part, e[:, u % 2, t], ALU.add).then_inc(merged, 1)
                    if u == 4:
                        split_low(two_kt(hhi)[0:2], two_kt(hlo)[0:2])
                split_low(two_kt(hhi)[2:4], two_kt(hlo)[2:4], 2)

            dve.memset(eps[:], EPS).then_inc(eps_set, 1)
            dve.memset(one[:], 1.0).then_inc(eps_set, 1)
            dve.wait_ge(params_in, w(params_in, 16 * N_PARAM))
            dve.wait_ge(consts_in, w(consts_in, 16 * N_CONST))
            dve.tensor_copy(half[:].rearrange("p a n -> p (a n)"), rtmp[:, 0, 0:3 * P])
            dve.scalar_tensor_tensor(lgt[:, 1], lgt[:, 0], -1.0, lgt[:, 0], ALU.mult, ALU.max).then_inc(lg_ready, 1)
            link(dve.tensor_tensor(dq[:], dq[:], dk[:], ALU.mult))
            dve.tensor_reduce(lam[:], dq[:], AX.X, ALU.add).then_inc(lam_dot, 1)
            dve.wait_ge(lg_exp, w(lg_exp))
            u, den, t1, t2_, acc = lgt[:, 2], lgt[:, 3], lgt[:, 4], lgt[:, 5], lgt[:, 3]
            link(dve.tensor_scalar(den, u, 2.0, None, ALU.add))
            link(dve.reciprocal(den, den))
            link(dve.tensor_tensor(t1, u, den, ALU.mult))
            link(dve.tensor_tensor(t2_, t1, t1, ALU.mult))
            link(dve.tensor_scalar(acc, t2_, 2.0 / 19, None, ALU.mult))
            for n in range(17, 1, -2):
                link(dve.scalar_tensor_tensor(acc, acc, 2.0 / n, t2_, ALU.add, ALU.mult))
            link(dve.scalar_tensor_tensor(acc, acc, 2.0, t1, ALU.add, ALU.mult))
            link(dve.tensor_scalar(t1, lgt[:, 0], 0.0, None, ALU.min))
            dve.tensor_tensor(lg[:].rearrange("p l d h -> p (l d h)"), t1, acc, ALU.subtract).then_inc(lg_ready, 1)
            dve.wait_ge(lam_exp, w(lam_exp))
            for l in range(DEPTH):
                start = 0.8 - 0.6 * math.exp(-0.3 * l)
                link(dve.tensor_tensor(nlam[:, l:l + 1], lam[:, 2 * l + 1:2 * l + 2], lam[:, 2 * l:2 * l + 1], ALU.subtract))
                link(dve.tensor_scalar(nlam[:, l:l + 1], nlam[:, l:l + 1], -start, None, ALU.add))
            dve.wait_ge(silu_c, w(silu_c))
            link(dve.tensor_copy(cThi[:], cT[:]))
            link(dve.tensor_tensor(cTlo[:], cT[:], cThi[:].bitcast(F32), ALU.subtract))
            pos = ang[:, 0, :, 0]
            link(dve.tensor_copy(pos, posi[:]))
            for t in range(TT):
                ins = dve.tensor_scalar(ang[:, 1, t], cst["inv2"][:], ang[:, 0, t, 0:1], None, ALU.mult)
            link(ins)
            big = 1.5 * 2.0 ** 23
            link(dve.tensor_scalar(ang[:, 3], ang[:, 1], 1.0 / (2 * math.pi), big, ALU.mult, ALU.add))
            link(dve.tensor_scalar(ang[:, 3], ang[:, 3], big, None, ALU.subtract))
            turn = [6.28125, 0.00193500518798828125, 2 * math.pi - 6.28125 - 0.00193500518798828125]
            src = ang[:, 1]
            for c in turn:
                link(dve.scalar_tensor_tensor(ang[:, 2], ang[:, 3], -c, src, ALU.mult, ALU.add))
                src = ang[:, 2]
            link(dve.tensor_scalar(ang[:, 2], ang[:, 2], math.pi, -math.pi, ALU.min, ALU.max))
            link(dve.scalar_tensor_tensor(ang[:, 3], ang[:, 2], -1.0, ang[:, 2], ALU.mult, ALU.max))
            dve.tensor_scalar(ang[:, 3], ang[:, 3], -1.0, math.pi / 2, ALU.mult, ALU.add).then_inc(ang_ready, 1)
            dve.wait_ge(tokens_in, w(tokens_in, 32))

            norm(cx)
            spread_conditions()

            for n, (is_x, l, full) in enumerate(PASSES):
                if not is_x:
                    dve.wait_ge(layer_in, w(layer_in, 16 * N_LAYER))
                    dve.wait_ge(evacuated, w(evacuated, 2 + 4))
                    link(dve.tensor_tensor(mod[:, 0:2 * D], mod[:, 0:2 * D], modb[:, 0:2 * D], ALU.add))
                    dve.scalar_tensor_tensor(mod[:, D:2 * D], mod[:, D:2 * D], 1.0, gpre[:], ALU.add, ALU.mult)\
                       .then_inc(mod_ready, 1)
                    dve.wait_ge(evacuated, w(evacuated, 2))
                    link(dve.tensor_tensor(mod[:, 2 * D:], mod[:, 2 * D:], modb[:, 2 * D:], ALU.add))
                    link(dve.tensor_tensor(mgate[:], mod[:, 2 * D:], gpost[:], ALU.mult))
                    dve.wait_ge(modT_ready, w(modT_ready, 4))
                a = 0 if is_x else 1
                turned_low(lambda k: modT[:, 1, k, a:a + 1], lambda k: modT[:, 0, k, a:a + 1])
                if n == 1:
                    residual(cx)
                if not is_x:
                    dve.wait_ge(tables_in, w(tables_in, 16 * N_TABLE))
                    for h in range(H1):
                        dve.wait_ge(decay_exp, w(decay_exp))
                        dve.tensor_tensor(e[:, h % 2, 0], e[:, h % 2, 0], dist[:, 2], ALU.mult)
                        link(dve.tensor_tensor(e[:, h % 2, 1], e[:, h % 2, 1], dist[:, 3], ALU.mult))
                        dve.tensor_tensor(decay[:, h], e[:, h % 2, 0], e[:, h % 2, 1], ALU.add).then_inc(decay_built, 1)
                    for d in range(4):
                        rc = cst["reach"][:].rearrange("p (a d) -> p a d", a=4)[:, d, :].unsqueeze(2).to_broadcast([P, 2, H1])
                        ins = dve.tensor_tensor(reachv[:, d], lg[:, l], rc, ALU.mult)
                    ins.then_inc(reach_arg, 1)
                if n == 2:
                    norm(x)
                dve.wait_ge(evacuated, w(evacuated, 2 * TT))
                if is_x:
                    for col in (RK, RQ):
                        dve.wait_ge(evacuated, w(evacuated, TT))
                        v = z[:, :, col:col + W].rearrange("p t (h c n) -> p t h c n", h=H1, c=2)
                        for t in range(TT):
                            cos, sin = (rope_r[:, t, c].unsqueeze(1).to_broadcast([P, H1, DK1 // 2]) for c in range(2))
                            temps = [rtmp[:, q, 0:W // 2].rearrange("p (h n) -> p h n", h=H1) for q in range(4)]
                            link(rotate(v[:, t, :, 0], v[:, t, :, 1], cos, sin, temps))
                    for col in (DKc, DQ):
                        dve.wait_ge(evacuated, w(evacuated, TT))
                        v = z[:, :, col:col + W].rearrange("p t (h c n) -> p t h c n", h=2 * H1, c=2)
                        for t in range(TT):
                            cos, sin = (rope_d[:, t, c].unsqueeze(1).to_broadcast([P, 2 * H1, DH // 2]) for c in range(2))
                            temps = [rtmp[:, q, 0:W // 2].rearrange("p (h n) -> p h n", h=2 * H1) for q in range(4)]
                            ins = rotate(v[:, t, :, 0], v[:, t, :, 1], cos, sin, temps)
                            if (col, t) == (DQ, TT - 1):
                                ins.then_inc(roped, 1)
                            else:
                                link(ins)
                    dve.wait_ge(evacuated, w(evacuated, 2 * TT))
                else:
                    dve.wait_ge(evacuated, w(evacuated, (6 if full else 4) * TT))
                    dve.wait_ge(reach_ready, w(reach_ready))
                    for h in range(H1):
                        if h >= 2:
                            dve.wait_ge(state_sum, w(state_sum))
                        for t in range(TT):
                            for d in range(2):
                                ins = dve.tensor_scalar(e[:, h % 2, t, d * DK1:(d + 1) * DK1],
                                                        z[:, t, RV + h * DK1:RV + (h + 1) * DK1],
                                                        reachv[:, 2 * t, d, h:h + 1], None, ALU.mult)
                        ins.then_inc(state_v, 1)
                    dve.wait_ge(state_sum, w(state_sum, 2))
                if not full:
                    continue
                for i in range(H1 + 1):
                    if i < H1:
                        dve.wait_ge(ret_scores, w(ret_scores))
                        dve.tensor_tensor(e[:, i % 2, 0], A[i % 2][:], decay[:, i], ALU.mult).then_inc(ret_weights, 1)
                    if i >= 1:
                        h = i - 1
                        if is_x:
                            dve.wait_ge(ret_cross, w(ret_cross))
                            cross = A[2 + h % 2][:].rearrange("p (t d n) -> p t d n", t=TT, d=2)
                            for t in range(TT):
                                ins = dve.tensor_scalar(e[:, h % 2, 1, t * P:(t + 1) * P], cross[:, t, 0],
                                                        reachv[:, 2 * t + 1, 0, h:h + 1], None, ALU.mult)
                            link(ins)
                            for t in range(TT):
                                part = e[:, h % 2, 1, t * P:(t + 1) * P]
                                ins = dve.scalar_tensor_tensor(part, cross[:, t, 1], reachv[:, 2 * t + 1, 1, h:h + 1], part,
                                                               ALU.mult, ALU.add)
                            link(ins)
                        dve.wait_ge(ret_out, w(ret_out))
                        inner = A[h % 2][:, 0:TT * P].rearrange("p (t n) -> p t n", t=TT)
                        res = o[:, 0, :, h * P:(h + 1) * P]
                        if is_x:
                            part = e[:, h % 2, 1, 0:TT * P].rearrange("p (t n) -> p t n", t=TT)
                            dve.tensor_tensor(res, inner, part, ALU.add).then_inc(ret_read, 1)
                        else:
                            dve.tensor_copy(res, inner).then_inc(ret_read, 1)

                def squares(b, at):
                    ob = o[:, b].rearrange("p t (h n) -> p (t h) n", h=H1)
                    sq = rtmp[:].rearrange("p a n -> p (a n)")[:, 0:TT * W].rearrange("p (q n) -> p q n", q=TT * H1)
                    link(dve.tensor_tensor(sq, ob, ob, ALU.mult))
                    return dve.tensor_reduce(ss[:, at:at + 8], sq, AX.X, ALU.add)

                dve.wait_ge(ret_read, w(ret_read, H1))
                link(squares(0, 0))
                m = H1 * TT
                nk = 2 * S if is_x else S

                def mix(i):
                    dve.wait_ge(diff_exp, w(diff_exp))
                    link(dve.reciprocal(rsum[:, i % 2], sums[:, i % 2]))
                    dve.tensor_scalar(e[:, i % 2, 0, 0:nk], e[:, i % 2, 0, 0:nk], rsum[:, i % 2, 0:1], None, ALU.mult)
                    link(dve.tensor_tensor(rsum[:, i % 2, 1:2], rsum[:, i % 2, 1:2], nlam[:, l:l + 1], ALU.mult))
                    dve.scalar_tensor_tensor(e[:, i % 2, 0, 0:nk], e[:, i % 2, 1, 0:nk], rsum[:, i % 2, 1:2], e[:, i % 2, 0, 0:nk],
                                             ALU.mult, ALU.add).then_inc(diff_mixed, 1)

                for i in range(m + 1):
                    if i < m:
                        dve.wait_ge(diff_scores, w(diff_scores))
                        for b in range(2):
                            ins = dve.reduce_max(mx[:, i % 2, b:b + 1], A[2 * (i % 2) + b][:, 0:nk], AX.X)
                        link(ins)
                        dve.tensor_scalar(nmx[:, i % 2], mx[:, i % 2], -DH ** -0.5, None, ALU.mult).then_inc(diff_max, 1)
                    if i >= 1:
                        mix(i - 1)
                dve.wait_ge(late_evacuated, w(late_evacuated, 4 * TT))
                for t in range(TT):
                    link(dve.bn_stats(bst[:, t], z[:, t, MV:MV + W]))
                    ins = dve.bn_aggr(bag[:, t], bst[:, t])
                ins.then_inc(var_ready, 1)
                dve.wait_ge(diff_read, w(diff_read, m))
                squares(2, 8).then_inc(ss_ready, 1)
                dve.wait_ge(dev_ready, w(dev_ready))
                link(dve.reciprocal(rstd[:, 0:TT], dev[:]))
                for t in range(TT):
                    ins = dve.tensor_scalar(z[:, t, MV:MV + W], z[:, t, MV:MV + W], bag[:, t, 0:1], rstd[:, t:t + 1],
                                            ALU.subtract, ALU.mult)
                    link(ins) if t < TT - 1 else ins.then_inc(mlp_vn, 1)
                dve.wait_ge(mlp_vn, w(mlp_vn))
                dve.wait_ge(rms_ready, w(rms_ready))
                link(dve.reciprocal(rstd[:], rms[:]))
                link(dve.tensor_scalar(rstd[:, 8:16], rstd[:, 8:16], 1.0 - (0.8 - 0.6 * math.exp(-0.3 * l)), None, ALU.mult))
                for b, at in ((0, 0), (2, 8)):
                    ob = o[:, b].rearrange("p t (h n) -> p (t h) n", h=H1)
                    ins = dve.tensor_tensor(ob, ob, rstd[:, at:at + 8].unsqueeze(2).to_broadcast([P, 8, P]), ALU.mult)
                link(ins)
                for b, gate in ((0, RG), (2, DG)):
                    dve.wait_ge(gates_ready, w(gates_ready))
                    dve.tensor_tensor(o[:, b], o[:, b], z[:, :, gate:gate + W], ALU.mult).then_inc(branches_ready, 1)
                for t in range(TT):
                    dve.wait_ge(mlp_mixed, w(mlp_mixed))
                    for b in range(4):
                        cols = slice(MU + b * P, MU + (b + 1) * P)
                        ins = dve.scalar_tensor_tensor(o[:, 1, t, b * P:(b + 1) * P], A[t][:, b * P:(b + 1) * P],
                                                       bs[:, l, b:b + 1], z[:, t, cols], ALU.add, ALU.mult)
                    link(ins)
                dve.wait_ge(late_evacuated, w(late_evacuated, TT))
                dve.tensor_tensor(o[:, 1], o[:, 1], z[:, :, MG:MG + W], ALU.mult).then_inc(branches_ready, 1)
                merge(True, (x, cx, None, None)[n])
                dve.wait_ge(out_evacuated, w(out_evacuated, 2 * TT))
                if n == 1:
                    spread_conditions()
                if is_x:
                    residual(x)
            dve.wait_ge(sin_ready, w(sin_ready))

            def layer(l):
                turned_low(lambda k: gT[:, 0, bass.ds(l, 1), k], None)
                token_scale()
                dve.wait_ge(evacuated, w(evacuated, 2 * TT + 8 * TT))
                for t in range(TT):
                    cos, sin = (rope_2[:, t, c] for c in range(2))
                    for col, nh in ((QC, 10), (QI, 5)):
                        v = z2[:, t, col:col + nh * DH].rearrange("p (h n) -> p h n", n=DH)
                        temps = [rt2[:, q, 0:nh * ROT].rearrange("p (h n) -> p h n", h=nh) for q in range(4)]
                        link(rotate(v[:, :, 0:ROT], v[:, :, ROT:2 * ROT], cos.unsqueeze(1).to_broadcast([P, nh, ROT]),
                                    sin.unsqueeze(1).to_broadcast([P, nh, ROT]), temps))
                for t in range(TT):
                    for c in range(2):
                        dve.tensor_copy(dup[:, t, 0:2, c * DH:(c + 1) * DH],
                                        z2[:, t, KC:KC + 2 * DH].rearrange("p (g n) -> p g n", g=2))
                        ins = dve.tensor_copy(dup[:, t, 2, c * DH:(c + 1) * DH], z2[:, t, KI:KI + DH])
                ins.then_inc(roped, 1)
                for t in range(TT):
                    ins = dve.tensor_tensor(fg[:, 0, t], z2[:, t, FL:FL + NF], bfg[:, bass.ds(l, 1), :].rearrange("p a n -> p (a n)"), ALU.add)
                link(ins)
                dve.scalar_tensor_tensor(fg[:, 1], fg[:, 0], -1.0, fg[:, 0], ALU.mult, ALU.max).then_inc(forget_in, 1)
                link(dve.tensor_scalar(fg[:, 2], fg[:, 0], 0.0, None, ALU.min))
                dve.wait_ge(forget_log, w(forget_log))
                dve.tensor_tensor(fg[:, 2], fg[:, 2], fg[:, 1], ALU.subtract).then_inc(forget_ready, 1)
                link(dve.tensor_scalar(wis[:], z2[:, :, WI:WI + NI], NI ** -0.5 * DH ** -0.5, None, ALU.mult))
                tiles = [slice(0, P), slice(P, 3 * P)]
                for h in range(NI):
                    dve.wait_ge(idx_relu, w(idx_relu))
                    for t in range(TT):
                        r = tmp[:, h % 2, h // 2, tiles[t]]
                        if h == 0:
                            ins = dve.tensor_scalar(work[:, tiles[t]], r, wis[:, t, h:h + 1], 0.0, ALU.mult, ALU.add)
                        else:
                            ins = dve.scalar_tensor_tensor(work[:, tiles[t]], r, wis[:, t, h:h + 1], work[:, tiles[t]],
                                                           ALU.mult, ALU.add)
                    link(ins)
                dve.tensor_tensor(work[:, 0:P], work[:, 0:P], causal16, ALU.add)
                link(dve.tensor_tensor(work[:, 2 * P:], work[:, 2 * P:], causal16, ALU.add))
                for r in range(TOPK // 8):
                    dve.sem_inc(topk_step, 1)
                    for t in range(TT):
                        ins = dve.max(mx8[:, t], work[:, tiles[t]])
                    link(ins)
                    dve.sem_inc(topk_step, 1)
                    for t in range(TT):
                        ins = dve.match_replace(work[:, tiles[t]], mx8[:, t], work[:, tiles[t]], TAKEN)
                    link(ins)
                dve.tensor_scalar(selb[:], work[:], TAKEN, NEG, ALU.not_equal, ALU.mult).then_inc(selected, 1)
                for i in range(H2):
                    dve.wait_ge(sb_log, w(sb_log))
                    dve.scalar_tensor_tensor(tmp[:, i % 2, 2], A[i % 2][:, 0:3 * P], 0.0, tmp[:, i % 2, 1],
                                             ALU.max, ALU.add).then_inc(sb_soft, 1)
                dve.wait_ge(heads_out, w(heads_out))
                for t in range(TT):
                    ins = dve.tensor_copy(o[:, 0, t], A[2 + t][:])
                ins.then_inc(heads_read, 1)
                for grp in range(2):
                    for i in range(H2):
                        dve.wait_ge(sm_scores, w(sm_scores))
                        dve.reduce_max(mx[:, i % 2, 0:1], A[i % 2][:, 0:P], AX.X)
                        link(dve.reduce_max(mx[:, i % 2, 1:2], A[i % 2][:, P:3 * P], AX.X))
                        dve.tensor_scalar(nmx[:, i % 2], mx[:, i % 2], -1.0, None, ALU.mult).then_inc(sm_max, 1)
                    dve.wait_ge(heads_out, w(heads_out))
                    dve.wait_ge(sm_exp, w(sm_exp, H2))
                    link(dve.reciprocal(hrec[:], hsum[:]))
                    for t in range(TT):
                        ins = dve.tensor_tensor(o[:, 1 + grp, t].rearrange("p (h n) -> p h n", h=H2),
                                                A[2 + t][:].rearrange("p (h n) -> p h n", h=H2),
                                                hrec[:, t].unsqueeze(2).to_broadcast([P, H2, DH]), ALU.mult)
                    ins.then_inc(heads_read, 1)
                merge(False)
                for c in range(D // CH):
                    for t in range(TT):
                        dve.wait_ge(out_projected, w(out_projected))
                        cols = slice(c * CH, (c + 1) * CH)
                        ins = dve.tensor_tensor(x[:, t, cols], x[:, t, cols], G[2 * c + t][:], ALU.add)
                    ins.then_inc(x_updated, 1)
                turned_low(lambda k: gT[:, 1, bass.ds(l, 1), k], None)
                token_scale()
                dve.wait_ge(rstd_ready, w(rstd_ready, 2))

                def square(j):
                    for t in range(TT):
                        dve.wait_ge(ff_relu, w(ff_relu))
                        dve.scalar_tensor_tensor(fsq[:, t], UP[j % 2][t][:], rstd[:, t:t + 1], frelu[:, t], ALU.mult, ALU.mult)\
                           .then_inc(ff_sq, 1)

                def squared_low(j):
                    for n, (hi, lo) in enumerate(zip(two_kt(uhi, 4), two_kt(ulo, 4))):
                        dve.wait_ge(split_hi, w(split_hi))
                        dve.tensor_tensor(lo, UP[j % 2][n][:], hi.bitcast(F32), ALU.subtract).then_inc(split_lo, 1)

                square(0)
                squared_low(0)
                square(1)
                with w.loop(FF // CH // 2 - 1, {ff_relu.name: 2 * TT, split_hi.name: 4}) as i:
                    for j in (1, 2):
                        squared_low(j)
                        square(j + 1)
                squared_low(FF // CH - 1)
                dve.wait_ge(ff_done, w(ff_done))
                for n in range(D // CH):
                    for t in range(TT):
                        cols = slice(n * CH, (n + 1) * CH)
                        ins = dve.tensor_tensor(x[:, t, cols], x[:, t, cols], DOWN[n][t][:], ALU.add)
                    ins.then_inc(x_updated, 1)

            with w.loop(DEPTH, LAYER_DVE) as l:
                layer(l)
            dve.wait_ge(rms_ready, w(rms_ready))
            link(dve.reciprocal(rstd[:, 0:TT], rms[:, 0:TT]))
            dve.wait_ge(final_in, w(final_in, 16))
            for t in range(TT):
                ins = dve.scalar_tensor_tensor(x[:, t], x[:, t], rstd[:, t:t + 1], gfin[:], ALU.mult, ALU.mult)
            ins.then_inc(out_ready, 1)

        @block.tensor
        def _(pe):
            w = Tally(pe)

            def product(bank, hi, lo, slot, kk, n, first, last):
                pe.matmul(bank, hi, whi[:, slot, kk, 0:n], start=first, stop=False)
                pe.matmul(bank, hi, wlo[:, slot, kk, 0:n], start=False, stop=False)
                return pe.matmul(bank, lo, whi[:, slot, kk, 0:n], start=False, stop=last)

            def slab(banks, hi, lo, s, n=CH, tiles=TT, ready=projected, fresh=False):
                pe.wait_ge(lo_ready, w(lo_ready))
                if fresh:
                    pe.wait_ge(h_split, w(h_split))
                for t in range(tiles):
                    for kk in range(SLAB_K):
                        k = s * SLAB_K + kk
                        cols = slice(t * P, (t + 1) * P)
                        ins = product(banks[t][:, 0:n], hi[:, k, cols], lo[:, k, cols], s, kk, n, k == 0, k == KT - 1)
                    if s == SLOTS - 1:
                        ins.then_inc(ready, 1)
                if s < SLOTS - 1:
                    ins.then_inc(weights_used, 1)

            def chunk(banks, hi, lo, n=CH, free=None, tiles=TT, ready=projected, fresh=False):
                for s in range(SLOTS):
                    if s == 0 and free is not None:
                        pe.wait_ge(free, w(free, tiles))
                    slab(banks, hi, lo, s, n, tiles, ready, fresh)

            def late_slab(n):
                c, s = divmod(n, SLOTS)
                if s == 0 and c >= 2:
                    pe.wait_ge(late_evacuated, w(late_evacuated, TT))
                slab(G[2 * (c % 2):2 * (c % 2) + 2], hhi, hlo, s, ready=late_projected)

            def turn_heads(blocks):
                count = (len(blocks) + 1) // 2
                for n in range(count):
                    if n >= 4:
                        pe.wait_ge(turned_copied, w(turned_copied))
                    for b, blk in enumerate(blocks[2 * n:2 * n + 2]):
                        for t in range(TT):
                            ins = pe.transpose(A[n % 4][:, b * S + t * P:b * S + (t + 1) * P], blk(t), ident[:])
                    ins.then_inc(turned, 1)
                pe.wait_ge(turned_copied, w(turned_copied, min(count, 4)))

            def turn_split(srcs, bank=0, settle=True):
                count = len(srcs) // 2
                for n in range(bank, bank + count):
                    if n >= 4:
                        pe.wait_ge(split_lo, w(split_lo))
                    for b in range(2):
                        for t in range(TT):
                            ins = pe.transpose(A[n % 4][:, b * S + t * P:b * S + (t + 1) * P], srcs[2 * (n - bank) + b](t),
                                               ident[:])
                    ins.then_inc(split_turned, 1)
                if settle:
                    pe.wait_ge(split_lo, w(split_lo, min(count, 4)))

            def turn_tokens(src, half_ready=None):
                for q in range(4):
                    if half_ready is not None and q % 2 == 0:
                        pe.wait_ge(half_ready, w(half_ready))
                    for b in range(2):
                        k = 2 * q + b
                        for t in range(TT):
                            ins = pe.transpose(HB[q][:, b * S + t * P:b * S + (t + 1) * P], src[:, t, k * P:(k + 1) * P], ident[:])
                    ins.then_inc(h_turned, 1)

            def pair_counts(n):
                return {lo_ready.name: SLOTS * n, evacuated.name: TT * n}

            def turn_branches():
                turn_split([lambda t, b=b, k=k: o[:, b, t, k * P:(k + 1) * P] for b in range(3) for k in range(4)], settle=False)

            def merge(ready):
                pe.wait_ge(split_lo, w(split_lo, 4))
                for u in range(6):
                    b = u % 3
                    for s in range(2):
                        slot = 2 * (u % 2) + s
                        pe.wait_ge(lo_ready, w(lo_ready))
                        for t in range(TT):
                            if s == 0 and u >= 2:
                                pe.wait_ge(merged, w(merged))
                            for kk in range(SLAB_K):
                                k = s * SLAB_K + kk
                                cols = slice(t * P, (t + 1) * P)
                                ins = product(G[2 * (u % 2) + t][:], ohi[:, b, k, cols], olo[:, b, k, cols], slot, kk, CH,
                                              k == 0, k == 3)
                            if s == 1:
                                ins.then_inc(branch_out, 1)
                        if s == 0:
                            ins.then_inc(weights_used, 1)
                    if u == 4:
                        turn_split([lambda t, k=k: y[:, t, k * P:(k + 1) * P] for k in range(4)], settle=False)
                pe.wait_ge(merged, w(merged, TT))
                pe.wait_ge(split_lo, w(split_lo, 2))
                for s in range(2):
                    slab(G[0:2], hhi, hlo, s, ready=ready)
                pe.wait_ge(merged, w(merged, TT))
                turn_split([lambda t, k=k: y[:, t, (4 + k) * P:(5 + k) * P] for k in range(4)], 2)
                for s in range(2, SLOTS):
                    slab(G[0:2], hhi, hlo, s, ready=ready)
                chunk(G[2:4], hhi, hlo, ready=ready)

            pe.wait_ge(consts_in, w(consts_in, 16 * N_CONST))
            pe.wait_ge(lo_ready, w(lo_ready, SLOTS))
            for n, (is_x, l, full) in enumerate(PASSES):
                if not is_x:
                    pe.wait_ge(cond_split, w(cond_split))
                    pe.sem_inc(evacuated, 2)
                    with w.loop(3, {lo_ready.name: 2 * SLOTS, evacuated.name: 2}) as i:
                        for p in range(2):
                            chunk(G[p:p + 1], hhi, hlo, free=evacuated, tiles=1)
                    pe.wait_ge(evacuated, w(evacuated, 2))
                    pe.wait_ge(mod_ready, w(mod_ready))
                    for q in range(4):
                        for b in range(4):
                            at = (4 * q + b) * P
                            ins = pe.transpose(G[q][:, b * P:(b + 1) * P], mod[:, at:at + P], ident[:])
                        ins.then_inc(mod_turned, 1)
                    pe.wait_ge(modT_ready, w(modT_ready, 4))
                pe.wait_ge(norm_ready, w(norm_ready, TT))
                turn_tokens(normed)
                pe.sem_inc(evacuated, 2 * TT)
                chunk(G[0:2], hhi, hlo, free=evacuated, fresh=True)
                chunk(G[2:4], hhi, hlo, free=evacuated)
                if not is_x:
                    if n > 0:
                        pe.wait_ge(x_updated, w(x_updated))
                    pe.wait_ge(tables_in, w(tables_in, 16 * N_TABLE))
                    for b in range(4):
                        ins = pe.transpose(A[0][:, b * P:(b + 1) * P], wsin[:, b], ident[:])
                    ins.then_inc(ws_turned, 1)
                with w.loop(2 if full else 1, pair_counts(2)) as i:
                    for p in range(2):
                        chunk(G[2 * p:2 * p + 2], hhi, hlo, free=evacuated)
                pe.wait_ge(evacuated, w(evacuated, 2 * TT))
                if not is_x:
                    pe.wait_ge(wsT_ready, w(wsT_ready))
                if n == 1:
                    pe.wait_ge(x_updated, w(x_updated))
                if is_x:
                    pe.wait_ge(roped, w(roped))
                cols = (RK, RQ, DKc, DQ) if full else (DKc,)
                turn_heads([lambda t, c=c, h=h: z[:, t, c + h * P:c + (h + 1) * P] for c in cols for h in range(H1)])
                rkT, rqT, dkT, dqT = (tT[:, a] for a in range(4))
                if not is_x:
                    for h in range(H1):
                        pe.wait_ge(state_v, w(state_v))
                        for t in range(TT):
                            ins = pe.matmul(A[h][:, 0:2 * DK1], z[:, t, RK + h * DK1:RK + (h + 1) * DK1],
                                            e[:, h % 2, t, 0:2 * DK1], start=t == 0, stop=t == TT - 1)
                        ins.then_inc(state_sum, 1)
                    pe.wait_ge(state_copied, w(state_copied, H1))
                    pe.wait_ge(turned_copied, w(turned_copied, TT))
                if not full:
                    continue
                for i in range(H1 + 1):
                    if i < H1:
                        if i >= 2:
                            pe.wait_ge(ret_read, w(ret_read))
                        for j in range(TT):
                            ins = pe.matmul(A[i % 2][:, j * S:(j + 1) * S], rkT[:, i, j * P:(j + 1) * P], rqT[:, i],
                                            start=True, stop=True)
                        ins.then_inc(ret_scores, 1)
                        if is_x:
                            for t in range(TT):
                                ins = pe.matmul(A[2 + i % 2][:, t * S:(t + 1) * S], rqT[:, i, t * P:(t + 1) * P],
                                                state[:, i].rearrange("p d n -> p (d n)"), start=True, stop=True)
                            ins.then_inc(ret_cross, 1)
                    late_slab(i)
                    if i >= 1:
                        h = i - 1
                        pe.wait_ge(ret_weights, w(ret_weights))
                        for t in range(TT):
                            for j in range(TT):
                                ins = pe.matmul(A[h % 2][:, t * P:(t + 1) * P], e[:, h % 2, 0, j * S + t * P:j * S + (t + 1) * P],
                                                z[:, j, RV + h * DK1:RV + (h + 1) * DK1], start=j == 0, stop=j == TT - 1)
                        ins.then_inc(ret_out, 1)
                pe.wait_ge(ret_read, w(ret_read, 2))
                m = H1 * TT
                late = H1 + 1
                for i in range(m + 1):
                    if i < m:
                        h, t = divmod(i, TT)
                        if i >= 2:
                            pe.wait_ge(diff_read, w(diff_read))
                        for b in range(2):
                            half_p = slice(b * DH, (b + 1) * DH)
                            bank = A[2 * (i % 2) + b]
                            keys = [cdkT, dkT] if is_x else [dkT]
                            for c, kT in enumerate(keys):
                                ins = pe.matmul(bank[:, c * S:(c + 1) * S], dqT[half_p, h, t * P:(t + 1) * P], kT[half_p, h],
                                                start=True, stop=True)
                        ins.then_inc(diff_scores, 1)
                        late_slab(late)
                        late += 1
                    if i >= 1:
                        j = i - 1
                        h = j // TT
                        nb = 4 if is_x else 2
                        pe.wait_ge(diff_mixed, w(diff_mixed))
                        for b in range(nb):
                            ins = pe.transpose(A[2 * (j % 2)][:, b * P:(b + 1) * P], e[:, j % 2, 0, b * P:(b + 1) * P], ident[:])
                        ins.then_inc(diff_turned, 1)
                        if j < LATE_DIFF:
                            late_slab(late)
                            late += 1
                        pe.wait_ge(diff_aT, w(diff_aT))
                        for b in range(nb):
                            val = cdv[:, b] if is_x and b < TT else z[:, b % TT, DV:DV + W]
                            ins = pe.matmul(A[2 * (j % 2) + 1][:, 0:P], aT[:, j % 2, b * P:(b + 1) * P], val[:, h * P:(h + 1) * P],
                                            start=b == 0, stop=b == nb - 1)
                        ins.then_inc(diff_out, 1)
                pe.wait_ge(diff_read, w(diff_read, 2))
                pe.wait_ge(mlp_vn, w(mlp_vn))
                for t in range(TT):
                    for b in range(4):
                        ins = pe.matmul(A[t][:, b * P:(b + 1) * P], wsT[:, b], z[:, t, MV + b * P:MV + (b + 1) * P],
                                        start=True, stop=True)
                    ins.then_inc(mlp_mixed, 1)
                while late < len(LATE) * SLOTS:
                    late_slab(late)
                    late += 1
                pe.wait_ge(late_evacuated, w(late_evacuated, 2 * TT))
                pe.wait_ge(branches_ready, w(branches_ready, 3))
                turn_branches()
                pe.sem_inc(evacuated, 2 * TT)
                with w.loop(3, pair_counts(2)) as i:
                    for p in range(2):
                        chunk(G[2 * p:2 * p + 2], hhi, hlo, free=evacuated)
                pe.wait_ge(evacuated, w(evacuated, 2 * TT))
                merge(projected)
                for c in range(D // CH):
                    pe.matmul(A[c][:], pick[:, 0 if is_x else 1], mgate[:, c * CH:(c + 1) * CH], start=True, stop=True)\
                      .then_inc(gate_spread, 1)
                pe.wait_ge(out_evacuated, w(out_evacuated, 2 * TT))

            pe.wait_ge(x_updated, w(x_updated))
            pe.wait_ge(gains_in, w(gains_in, 16))

            def layer(l):
                turn_tokens(x)
                pe.sem_inc(evacuated, 2 * TT)
                chunk(G[0:2], hhi, hlo, free=evacuated, fresh=True)
                for p in (1, 0, 1, 0):
                    chunk(G[2 * p:2 * p + 2], hhi, hlo, free=evacuated)
                for n, (col, width) in enumerate(MID, 1):
                    chunk(G[2 * (n % 2):2 * (n % 2) + 2], hhi, hlo, width, free=evacuated)
                pe.wait_ge(evacuated, w(evacuated, 2 * TT))
                pe.wait_ge(roped, w(roped))

                def head_block(c, n):
                    return lambda t: z2[:, t, c + n * P:c + (n + 1) * P]

                blocks = [head_block(c, n) for c in (QA, KA, QB, KB, QC) for n in range(4)]
                blocks += [head_block(QI, n) for n in range(2)] + [lambda t, n=n: dup[:, t, n] for n in range(3)]
                turn_heads(blocks)
                qa, ka, qb, kb, qc, qi = (t2[:, 4 * a:4 * a + 4] for a in range(6))
                kc, ki = t2[:, 22:24], t2[:, 24]

                def rows(h):
                    return slice((h % 2) * DH, (h % 2 + 1) * DH)

                def scores(bank, q, k, h):
                    pe.matmul(bank[:, 0:P], q[rows(h), 0:P], k[rows(h), 0:P], start=True, stop=False, skip_group_check=True)
                    return pe.matmul(bank[:, P:3 * P], q[rows(h), P:S], k[rows(h), 0:S], start=False, stop=False,
                                     skip_group_check=True)

                for h in range(NI):
                    pe.matmul(A[h][:, 0:P], qi[rows(h), h // 2, 0:P], ki[rows(h), 0:P], start=True, stop=True)
                    pe.matmul(A[h][:, P:3 * P], qi[rows(h), h // 2, P:S], ki[rows(h), 0:S], start=True, stop=True)\
                      .then_inc(idx_dots, 1)
                pe.wait_ge(idx_relu, w(idx_relu, NI))
                pe.wait_ge(forget_ready, w(forget_ready))
                pe.matmul(A[0][0:NF, 0:S], fg[:, 2, 0], upto[:, 0:S], start=True, stop=False, skip_group_check=True)
                pe.matmul(A[0][0:NF, P:S], fg[:, 2, 1], upto[:, 0:P], start=False, stop=True, skip_group_check=True).then_inc(cum_out, 1)
                pe.wait_ge(cum_copied, w(cum_copied))
                for late in range(LATE_TOPK):
                    late_slab(late)
                late = LATE_TOPK
                for i in range(H2 + 2):
                    if i >= 2:
                        j = i - 2
                        pe.wait_ge(sb_weights, w(sb_weights))
                        v = [z2[:, s, VA + j * DH:VA + (j + 1) * DH] for s in range(TT)]
                        cols = slice(j * DH, (j + 1) * DH)
                        pe.matmul(A[2][:, cols], tmp[:, j % 2, 3, 0:P], v[0], start=True, stop=True)
                        pe.matmul(A[3][:, cols], tmp[:, j % 2, 3, P:2 * P], v[0], start=True, stop=False)
                        ins = pe.matmul(A[3][:, cols], tmp[:, j % 2, 3, 2 * P:], v[1], start=False, stop=True)
                        if j == H2 - 1:
                            ins.then_inc(heads_out, 1)
                    if i < H2:
                        bank, q, k = A[i % 2], qa[:, i // 2], ka[:, i // 2]
                        pe.matmul(bank[:, 0:S], k[rows(i), 0:P], q[rows(i), 0:S], start=True, stop=False, skip_group_check=True)
                        pe.matmul(bank[:, S:3 * P], k[rows(i), P:S], q[rows(i), P:S], start=False, stop=False, skip_group_check=True)
                        pe.matmul(bank[:, 0:P], ident16, strict16, start=False, stop=False, skip_group_check=True)
                        pe.matmul(bank[:, S:3 * P], ident16, strict16, start=False, stop=True, skip_group_check=True)\
                          .then_inc(sb_scores, 1)
                        late_slab(late)
                        late += 1
                    if 1 <= i <= H2:
                        j = i - 1
                        pe.wait_ge(sb_soft, w(sb_soft))
                        pe.matmul(A[j % 2][:, 0:3 * P], later[:], tmp[:, j % 2, 2], start=False, stop=False, skip_group_check=True)
                        pe.matmul(A[j % 2][:, P:S], every[:], tmp[:, j % 2, 2, S:3 * P], start=False, stop=True,
                                  skip_group_check=True).then_inc(sb_cum, 1)
                pe.wait_ge(heads_read, w(heads_read))
                for grp in range(2):
                    for i in range(H2 + 2):
                        if i >= 2:
                            j = i - 2
                            pe.wait_ge(sm_copied, w(sm_copied))
                            col = VB + j * DH if grp == 0 else VC + (j // 4) * DH
                            v = [z2[:, s, col:col + DH] for s in range(TT)]
                            cols = slice(j * DH, (j + 1) * DH)
                            pe.matmul(A[2][:, cols], tmp[:, j % 2, 1, 0:P], v[0], start=True, stop=True)
                            pe.matmul(A[3][:, cols], tmp[:, j % 2, 1, P:2 * P], v[0], start=True, stop=False)
                            ins = pe.matmul(A[3][:, cols], tmp[:, j % 2, 1, 2 * P:], v[1], start=False, stop=True)
                            if j == H2 - 1:
                                ins.then_inc(heads_out, 1)
                        if i < H2:
                            bank = A[i % 2]
                            if grp == 0:
                                scores(bank, qb[:, i // 2], kb[:, i // 2], i)
                                pe.matmul(bank[:, 0:P], esel[0:NF, i], negc[0:NF, 0:P], start=False, stop=False, skip_group_check=True)
                                pe.matmul(bank[:, P:3 * P], esel[0:NF, i], negc[0:NF, 0:S], start=False, stop=False, skip_group_check=True)
                            else:
                                if i == 0:
                                    pe.wait_ge(selected, w(selected))
                                scores(bank, qc[:, i // 2], kc[:, i // 4], i)
                                pe.matmul(bank[:, 0:3 * P], ident16, selb[:], start=False, stop=False, skip_group_check=True)
                            pe.matmul(bank[:, 0:P], ident16, causal16, start=False, stop=False, skip_group_check=True)
                            pe.matmul(bank[:, 2 * P:3 * P], ident16, causal16, start=False, stop=True, skip_group_check=True)\
                              .then_inc(sm_scores, 1)
                            if i < LATE_SM[grp]:
                                late_slab(late)
                                late += 1
                        if 1 <= i <= H2:
                            j = i - 1
                            pe.wait_ge(sm_exp, w(sm_exp))
                            for b in range(3):
                                ins = pe.transpose(A[j % 2][:, b * P:(b + 1) * P], tmp[:, j % 2, 0, b * P:(b + 1) * P], ident[:])
                            ins.then_inc(sm_turned, 1)
                    pe.wait_ge(heads_read, w(heads_read))
                pe.wait_ge(late_evacuated, w(late_evacuated, 2 * TT))
                turn_branches()
                merge(out_projected)
                turn_tokens(x, x_updated)

                def up(j, slabs, fresh=False):
                    for s in slabs:
                        slab(UP[j % 2], hhi, hlo, s, fresh=fresh)

                def turn_squared(j):
                    pe.wait_ge(ff_sq, w(ff_sq, TT))
                    for n in range(2):
                        for b in range(2):
                            for t in range(TT):
                                k = 2 * n + b
                                ins = pe.transpose(UP[j % 2][n][:, b * S + t * P:b * S + (t + 1) * P],
                                                   fsq[:, t, k * P:(k + 1) * P], ident[:])
                        ins.then_inc(split_turned, 1)

                def down(first, last):
                    for n in range(D // CH):
                        for s in range(2):
                            pe.wait_ge(lo_ready, w(lo_ready))
                            if n == 0:
                                pe.wait_ge(split_lo, w(split_lo))
                            for t in range(TT):
                                for kk in range(SLAB_K):
                                    k = s * SLAB_K + kk
                                    cols = slice(t * P, (t + 1) * P)
                                    ins = product(DOWN[n][t][:], uhi[:, k, cols], ulo[:, k, cols], 2 * n + s, kk, CH,
                                                  first and k == 0, last and k == 3)
                            end = last and n == D // CH - 1 and s == 1
                            ins.then_inc(ff_done if end else weights_used, 1)

                def step(j):
                    up(j + 1, range(0, 2))
                    turn_squared(j)
                    up(j + 1, range(2, SLOTS))
                    down(j == 0, False)

                up(0, range(SLOTS), True)
                step(0)
                per = {lo_ready.name: 4 * SLOTS, ff_sq.name: 2 * TT, split_lo.name: 4}
                with w.loop(FF // CH // 2 - 1, per) as i:
                    step(1)
                    step(2)
                turn_squared(FF // CH - 1)
                down(False, True)
                pe.wait_ge(x_updated, w(x_updated, 2))

            with w.loop(DEPTH, LAYER_PE) as l:
                layer(l)


LAYER_ACT = {'raw_full0': 576, 'raw_full1': 576, 'raw_full2': 576, 'raw_full3': 576, 'act_step': 20, 'weights_used': 112, 'projected': 32, 'h_turned': 8, 'turned': 13, 'late_projected': 14, 'late_evacuated': 14, 'split_turned': 26, 'branch_out': 12, 'x_updated': 4, 'rstd_ready': 2, 'idx_dots': 4, 'forget_in': 1, 'forget_exp': 1, 'cum_out': 1, 'selected': 1, 'sb_scores': 8, 'sb_cum': 8, 'sm_max': 16, 'sm_turned': 16, 'heads_read': 3, 'out_projected': 4}
LAYER_DVE = {'dve_step': 58, 'rms_ready': 2, 'evacuated': 20, 'h_high': 8, 'gates_ready': 6, 'split_hi': 26, 'branch_out': 12, 'forget_log': 1, 'idx_relu': 4, 'sb_log': 8, 'heads_out': 3, 'sm_scores': 16, 'sm_exp': 16, 'out_projected': 4, 'rstd_ready': 2, 'ff_relu': 16, 'ff_done': 1}
LAYER_PE = {'lo_ready': 144, 'evacuated': 20, 'h_split': 8, 'turned_copied': 13, 'late_evacuated': 14, 'split_lo': 26, 'merged': 12, 'x_updated': 4, 'roped': 1, 'idx_relu': 4, 'forget_ready': 1, 'cum_copied': 1, 'sb_soft': 8, 'sb_weights': 8, 'heads_read': 3, 'sm_exp': 16, 'sm_copied': 16, 'selected': 1, 'ff_sq': 16}

_INS = ["x", "c", "ctx", "c_ctx", "w_mod", "b_mod", "g_pre", "g_post", "w_in", "ret_decay_logit", "mlp_w_s", "mlp_b_s",
        "diff_lambda_q", "diff_lambda_k", "w_branch_out", "w_out", "positions_2", "g_mix_2", "w_in_2", "b_forget_2",
        "w_branch_2", "w_out_2", "g_mlp_2", "w_up_2", "w_down_2", "g_final_2"]


def kernel(**inputs):
    import concourse.bacc as bacc
    from concourse.bass_utils import run_bass_kernel_spmd

    nc = bacc.Bacc("TRN2", target_bir_lowering=False, num_devices=1)
    parts, dist, head, half = constants()
    arrays = {n: np.ascontiguousarray(inputs[n]) for n in _INS}
    arrays |= {"k_" + n: a for n, a in parts.items()} | {"k_dist": dist, "k_head": head, "k_half": half}
    arrays = {"in_" + n: np.ascontiguousarray(a) for n, a in arrays.items()}
    g = {n[3:]: nc.dram_tensor(n, a.shape, mybir.dt.from_np(a.dtype), kind="ExternalInput").ap() for n, a in arrays.items()}
    out = nc.dram_tensor("result", (1, S, D), F32, kind="ExternalOutput").ap()
    build(nc, g, out)
    return run_bass_kernel_spmd(nc, [arrays], core_ids=[0]).results[0]["result"]
```
